# Optimizing a Trainium2 kernel written in Bass

```python
import jax, jax.numpy as jnp
from jax import lax
import numpy as np

D_MODEL = 1024
BATCH = 1
SEQ = 256
DEPTH = 2

N_A_LAYERS = DEPTH // 2
N_B_LAYERS = DEPTH - N_A_LAYERS
EPS = 1e-6

HG_EXPAND = 128
HG_HEADS = D_MODEL // HG_EXPAND
HG_DK = D_MODEL // HG_HEADS
HG_DV = D_MODEL // HG_HEADS
HG_CHUNK = 64

DIL_GROUPS = ((128, 1), (512, 4), (2048, 16))
N_GROUPS = len(DIL_GROUPS)
HEAD_DIM = 128
KV_PER_GROUP = 2
Q_PER_KV = 2
Q_WIDTH = N_GROUPS * KV_PER_GROUP * Q_PER_KV * HEAD_DIM
KV_WIDTH = N_GROUPS * KV_PER_GROUP * HEAD_DIM
ATT_OUT_WIDTH = KV_PER_GROUP * Q_PER_KV * HEAD_DIM
ROT_DIM = HEAD_DIM // 4
ROPE_THETA = 500000.0
Q_BLOCK = 128

PEER_HEADS = 8
PEER_TOPK = 16
N_KEYS = 128
N_EXPERTS = N_KEYS * N_KEYS
PEER_DKEY = 256
PEER_CHUNK = 128

kernel_name = "yoco_hgrn2_dilated_attn_peer"

def rmsnorm(x, g):
    xf = x.astype(jnp.float32)
    y = xf * lax.rsqrt(jnp.mean(xf * xf, axis=-1, keepdims=True) + EPS)
    return (y * g.astype(jnp.float32)).astype(x.dtype)

def rope_partial(x, pos):
    half = ROT_DIM // 2
    inv = ROPE_THETA ** (-jnp.arange(half, dtype=jnp.float32) * 2.0 / ROT_DIM)
    ang = pos.astype(jnp.float32)[:, None] * inv[None, :]
    ang = ang.reshape((1, pos.shape[0]) + (1,) * (x.ndim - 3) + (half,))
    cos, sin = jnp.cos(ang), jnp.sin(ang)
    xr = x[..., :ROT_DIM].astype(jnp.float32)
    x1, x2 = xr[..., :half], xr[..., half:]
    rot = jnp.concatenate([x1 * cos - x2 * sin, x2 * cos + x1 * sin], axis=-1)
    return jnp.concatenate([rot.astype(x.dtype), x[..., ROT_DIM:]], axis=-1)

def hgrn2_mixer(h, norm_g, w_in, lb, out_g, w_out):
    B, S, _ = h.shape
    nc = S // HG_CHUNK
    xn = rmsnorm(h, norm_g)
    q, fr, i, g = jnp.split(xn @ w_in, 4, axis=-1)
    q = jax.nn.silu(q.astype(jnp.float32))
    f = lb + (1.0 - lb) * jax.nn.sigmoid(fr.astype(jnp.float32))
    k = 1.0 - f
    logf = jnp.log(f)

    def to_chunks(t, d):
        return t.astype(jnp.float32).reshape(B, nc, HG_CHUNK, HG_HEADS, d).transpose(1, 0, 3, 2, 4)

    qc, kc, gc = to_chunks(q, HG_DK), to_chunks(k, HG_DK), to_chunks(logf, HG_DK)
    vc = to_chunks(i, HG_DV)
    causal = jnp.tril(jnp.ones((HG_CHUNK, HG_CHUNK), dtype=bool))

    def step(state, inp):
        qt, kt, vt, gt = inp
        b = jnp.cumsum(gt, axis=-2)
        inter = jnp.einsum('bhcd,bhde->bhce', qt * jnp.exp(b), state)
        diff = b[:, :, :, None, :] - b[:, :, None, :, :]
        decay = jnp.exp(jnp.where(causal[None, None, :, :, None], diff, -jnp.inf))
        scores = jnp.einsum('bhid,bhijd,bhjd->bhij', qt, decay, kt)
        intra = jnp.einsum('bhij,bhje->bhie', scores, vt)
        b_last = b[:, :, -1:, :]
        new_state = jnp.exp(b_last[:, :, 0, :])[..., None] * state + jnp.einsum(
            'bhjd,bhje->bhde', kt * jnp.exp(b_last - b), vt)
        return new_state, inter + intra

    s0 = jnp.zeros((B, HG_HEADS, HG_DK, HG_DV), jnp.float32)
    _, o = lax.scan(step, s0, (qc, kc, vc, gc))
    o = o.transpose(1, 0, 3, 2, 4).reshape(B, S, HG_HEADS, HG_DV)
    o = rmsnorm(o, out_g) * jax.nn.silu(g.astype(jnp.float32).reshape(B, S, HG_HEADS, HG_DV))
    return o.reshape(B, S, D_MODEL).astype(h.dtype) @ w_out

def shared_kv(h, kv_norm, w_kv, k_norm):
    B, S, _ = h.shape
    pos = jnp.arange(S)
    k, v = jnp.split(rmsnorm(h, kv_norm) @ w_kv, 2, axis=-1)
    k = k.reshape(B, S, N_GROUPS, KV_PER_GROUP, HEAD_DIM)
    v = v.reshape(B, S, N_GROUPS, KV_PER_GROUP, HEAD_DIM)
    k = rope_partial(rmsnorm(k, k_norm), pos)
    return k, v

def dilated_attention(h, k, v, norm_g, w_q, q_norm, w_o):
    B, S, _ = h.shape
    pos = jnp.arange(S)
    q = (rmsnorm(h, norm_g) @ w_q).reshape(B, S, N_GROUPS, KV_PER_GROUP, Q_PER_KV, HEAD_DIM)
    q = rope_partial(rmsnorm(q, q_norm), pos)
    scale = HEAD_DIM ** -0.5

    def block(s0):
        t = s0 + jnp.arange(Q_BLOCK)
        qb = lax.dynamic_slice_in_dim(q, s0, Q_BLOCK, axis=1)
        outs, lses = [], []
        for gi, (w, d) in enumerate(DIL_GROUPS):
            m = jnp.arange(w // d + 1)
            idx = t[:, None] - d * m[None, :]
            valid = idx >= 0
            idxc = jnp.maximum(idx, 0)
            kg = jnp.take(k[:, :, gi], idxc, axis=1)
            vg = jnp.take(v[:, :, gi], idxc, axis=1)
            s = jnp.einsum('bqkrd,bqmkd->bqkrm', qb[:, :, gi], kg).astype(jnp.float32) * scale
            s = jnp.where(valid[None, :, None, None, :], s, -jnp.inf)
            lse = jax.nn.logsumexp(s, axis=-1)
            p = jnp.exp(s - lse[..., None])
            o = jnp.einsum('bqkrm,bqmkd->bqkrd', p.astype(vg.dtype), vg)
            outs.append(o.astype(jnp.float32))
            lses.append(lse)
        alpha = jax.nn.softmax(jnp.stack(lses, axis=0), axis=0)
        comb = jnp.sum(alpha[..., None] * jnp.stack(outs, axis=0), axis=0)
        return comb.astype(h.dtype)

    starts = jnp.arange(S // Q_BLOCK) * Q_BLOCK
    o = lax.map(block, starts)
    o = jnp.moveaxis(o, 0, 1).reshape(B, S, ATT_OUT_WIDTH)
    return o @ w_o

def peer(h, norm_g, w_q, sub_keys, u, v):
    B, S, D = h.shape
    T = B * S
    half = PEER_DKEY // 2
    xn = rmsnorm(h, norm_g).reshape(T, D)
    q = (xn @ w_q).reshape(T, PEER_HEADS, PEER_DKEY)
    s1 = jnp.einsum('thd,nd->thn', q[..., :half], sub_keys[0]).astype(jnp.float32)
    s2 = jnp.einsum('thd,nd->thn', q[..., half:], sub_keys[1]).astype(jnp.float32)
    v1, i1 = lax.top_k(s1, PEER_TOPK)
    v2, i2 = lax.top_k(s2, PEER_TOPK)
    cand = (v1[..., :, None] + v2[..., None, :]).reshape(T, PEER_HEADS, PEER_TOPK * PEER_TOPK)
    cs, ci = lax.top_k(cand, PEER_TOPK)
    e1 = jnp.take_along_axis(i1, ci // PEER_TOPK, axis=-1)
    e2 = jnp.take_along_axis(i2, ci % PEER_TOPK, axis=-1)
    experts = (e1 * N_KEYS + e2).reshape(T, PEER_HEADS * PEER_TOPK)
    gates = jax.nn.softmax(cs, axis=-1).reshape(T, PEER_HEADS * PEER_TOPK)

    def chunk(args):
        xc, ec, gc = args
        uc = jnp.take(u, ec, axis=0)
        z = jnp.einsum('td,ted->te', xc, uc).astype(jnp.float32)
        act = jax.nn.gelu(z) * gc
        vc = jnp.take(v, ec, axis=0)
        return jnp.einsum('te,ted->td', act.astype(vc.dtype), vc)

    nch = T // PEER_CHUNK
    out = lax.map(chunk, (xn.reshape(nch, PEER_CHUNK, D),
                          experts.reshape(nch, PEER_CHUNK, -1),
                          gates.reshape(nch, PEER_CHUNK, -1)))
    return out.reshape(B, S, D).astype(h.dtype)

def setup_inputs(seed: int = 0) -> dict:
    key = jax.random.key(seed)
    ks = jax.random.split(key, 20)
    nrm = jax.random.normal
    D = D_MODEL
    return {
        "x": nrm(ks[0], (BATCH, SEQ, D), jnp.float32),
        "hgrn_norm": 1.0 + 0.02 * nrm(ks[1], (N_A_LAYERS, D), jnp.float32),
        "hgrn_w_in": nrm(ks[2], (N_A_LAYERS, D, 4 * D), jnp.float32) * D ** -0.5,
        "hgrn_lb_logits": 0.1 * nrm(ks[3], (N_A_LAYERS + 1, D), jnp.float32),
        "hgrn_out_norm": 1.0 + 0.02 * nrm(ks[4], (N_A_LAYERS, HG_DV), jnp.float32),
        "hgrn_w_out": nrm(ks[5], (N_A_LAYERS, D, D), jnp.float32) * D ** -0.5,
        "kv_norm": 1.0 + 0.02 * nrm(ks[6], (D,), jnp.float32),
        "w_kv": nrm(ks[7], (D, 2 * KV_WIDTH), jnp.float32) * D ** -0.5,
        "k_norm": 1.0 + 0.02 * nrm(ks[8], (HEAD_DIM,), jnp.float32),
        "attn_norm": 1.0 + 0.02 * nrm(ks[9], (N_B_LAYERS, D), jnp.float32),
        "w_q": nrm(ks[10], (N_B_LAYERS, D, Q_WIDTH), jnp.float32) * D ** -0.5,
        "q_norm": 1.0 + 0.02 * nrm(ks[11], (N_B_LAYERS, HEAD_DIM), jnp.float32),
        "w_o": nrm(ks[12], (N_B_LAYERS, ATT_OUT_WIDTH, D), jnp.float32) * ATT_OUT_WIDTH ** -0.5,
        "ffn_norm": 1.0 + 0.02 * nrm(ks[13], (DEPTH, D), jnp.float32),
        "peer_w_q": nrm(ks[14], (DEPTH, D, PEER_HEADS * PEER_DKEY), jnp.float32) * D ** -0.5,
        "peer_sub_keys": nrm(ks[15], (DEPTH, 2, N_KEYS, PEER_DKEY // 2), jnp.float32) * (PEER_DKEY // 2) ** -0.5,
        "peer_u": nrm(ks[16], (DEPTH, N_EXPERTS, D), jnp.float32) * D ** -0.5,
        "peer_v": nrm(ks[17], (DEPTH, N_EXPERTS, D), jnp.float32) * PEER_HEADS ** -0.5,
    }

def reference(x, hgrn_norm, hgrn_w_in, hgrn_lb_logits, hgrn_out_norm, hgrn_w_out,
              kv_norm, w_kv, k_norm, attn_norm, w_q, q_norm, w_o,
              ffn_norm, peer_w_q, peer_sub_keys, peer_u, peer_v):
    lbs = jnp.cumsum(jax.nn.softmax(hgrn_lb_logits.astype(jnp.float32), axis=0), axis=0)
    h = x
    k_sh, v_sh = None, None
    for layer in range(DEPTH):
        if layer < N_A_LAYERS:
            h = h + hgrn2_mixer(h, hgrn_norm[layer], hgrn_w_in[layer], lbs[layer],
                                hgrn_out_norm[layer], hgrn_w_out[layer]).astype(h.dtype)
        else:
            if layer == N_A_LAYERS:
                k_sh, v_sh = shared_kv(h, kv_norm, w_kv, k_norm)
            j = layer - N_A_LAYERS
            h = h + dilated_attention(h, k_sh, v_sh, attn_norm[j], w_q[j],
                                      q_norm[j], w_o[j]).astype(h.dtype)
        h = h + peer(h, ffn_norm[layer], peer_w_q[layer], peer_sub_keys[layer],
                     peer_u[layer], peer_v[layer]).astype(h.dtype)
    return h


_drawn_inputs = setup_inputs


def setup_inputs(seed=0):
    import zlib

    import numpy as np

    out = dict(_drawn_inputs(seed))
    spreads = {}
    factors = {'kv_norm': 5.058, 'k_norm': 6.104, 'attn_norm': 7.297, 'q_norm': 6.089}
    for name, (base, spread) in spreads.items():
        noise = np.random.default_rng([zlib.crc32(name.encode()), seed]).standard_normal(out[name].shape)
        drawn = base * np.exp(spread * noise) if base else spread * noise
        out[name] = __import__('jax').numpy.asarray(drawn.astype(out[name].dtype))
    for name, factor in factors.items():
        out[name] = (out[name] * factor).astype(out[name].dtype)
    return out
```

```python
import concourse.bass as bass
from concourse import mybir
from contextlib import ExitStack

F32 = mybir.dt.float32
U32 = mybir.dt.uint32
U8 = mybir.dt.uint8
ALU = mybir.AluOpType
ACT = mybir.ActivationFunctionType
AX = mybir.AxisListType

P = 128
D = 1024
KT_D = D // P
TILES = 2
EPS = 1e-6
HG_HEADS = D // P
LEVELS = 7
HD = 128
N_GROUPS, KV_PER_GROUP, Q_PER_KV = 3, 2, 2
NQH = N_GROUPS * KV_PER_GROUP * Q_PER_KV
NKH = N_GROUPS * KV_PER_GROUP
NJH = KV_PER_GROUP * Q_PER_KV
HALF_ROT = HD // 8
HEADS = 8
TOPK = 16
N_KEYS = 128
N_EXPERTS = N_KEYS * N_KEYS
PHASES = 4
RING = 8
DIAGS = 4
GROUPS = TOPK // RING
SLOTS = HEADS * TOPK
WRING = 4
CHUNK = 2048
GELU_CUBE = 0.044715
GELU_SCALE = 2.0 * 0.7978845608028654
LOWEST = -3.0e38
CONSTS = 13
ROUTE_LINKS = 26
ROW_LINKS = 6

W_IN, W_OUT, W_KV, W_Q, W_O, W_P0, W_P1, W_END = 0, 16, 20, 26, 32, 34, 42, 50
GAINS = 5
GAIN_HG, GAIN_KV, GAIN_ATT, GAIN_F0 = range(4)
GAIN_F1 = GAIN_HG
CUTS = [1] * HEADS
PIECES = [2, 2, 2, 2, 1, 1, 1, 1]


class Chain:

    def __init__(self, engine, sem):
        self.engine, self.sem, self.n, self.base, self.step = engine, sem, 0, 0, None

    def tick(self, ins):
        self.n += 1
        ins.then_inc(self.sem, 1)

    def link(self, ins):
        self.tick(ins)
        self.engine.wait_ge(self.sem, self.base + self.n if self.step is None else self.step + (self.base + self.n))

    def link_apart(self, ins, tick):
        self.link(ins)
        self.engine.sem_inc(tick, 1)

    def enter(self, i, per):
        self.base, self.n, self.per, self.step = self.base + self.n, 0, per, i * per

    def leave(self, count):
        assert self.n == self.per, self.n
        self.base, self.n, self.step = self.base + count * self.per, 0, None


class Count:

    def __init__(self):
        self.chunks = 0
        self.banks = 0
        self.transposes = 0
        self.pairs = 0
        self.met = {}

    def next(self, name, n=1):
        self.met[name] = self.met.get(name, 0) + n
        return self.met[name]


def build(nc, x_d, wall_d, gains_d, lb_d, headg_d, rope_d, amask_d, lmask_d, ident_d, iota_d, skt_d,
          u_d, v_d, out_d):
    ctx = ExitStack()
    with ctx:
        def sb(name, shape, dt=F32):
            return ctx.enter_context(nc.sbuf_tensor(name, shape, dt))

        def sem(name):
            return ctx.enter_context(nc.semaphore(name))

        u_ring = sb("u_ring", [P, RING, D])
        v_ring = sb("v_ring", [P, RING, D])
        w_ring = sb("w_ring", [P, WRING, CHUNK])
        h = sb("h", [P, TILES, D])
        xp = sb("xp", [P, TILES, D])
        xn = sb("xn", [P, D])
        xT = sb("xT", [P, KT_D, P])
        gains = sb("gains", [P, 4, D])
        headg = sb("headg", [P, 3, HD])
        lbl = sb("lbl", [P, 2, HG_HEADS])
        lb = sb("lb", [P, HG_HEADS])
        lb1 = sb("lb1", [P, HG_HEADS])
        rope = sb("rope", [P, TILES, 2, HALF_ROT])
        lmask = sb("lmask", [P, LEVELS + 1, P], U8)
        ident = sb("ident", [P, P])
        iota = sb("iota", [P, TOPK])
        ones = sb("ones", [P, P])
        zero = sb("zero", [P, P])
        skt = sb("skt", [P, 2, 2, N_KEYS])
        idx_all = sb("idx_all", [P, PHASES * SLOTS], U32)
        gate_all = sb("gate_all", [P, PHASES * SLOTS])
        arena = sb("arena", [P, 12544])

        def part(first, size):
            return arena[:, first:first + size]

        qT, kT, bT, eT, qe, ke, vi, gi, on, sT, state, raw = (part(n * D, D) for n in range(12))
        keyT = part(0, NKH * TILES * P).rearrange("p (n t) -> p n t", n=NKH)
        val = part(1536, TILES * NKH * HD).rearrange("p (t n) -> p t n", t=TILES)
        amask = part(3072, 1152)
        qs = part(4608, NQH * HD)
        qhT = part(6144, NQH * P).rearrange("p (n t) -> p n t", n=NQH)
        ks = part(7680, NKH * HD)
        pr = part(8448, 768)
        prT = part(9216, 768).rearrange("p (n t) -> p n t", n=6)
        oat = part(9984, 512)
        sq = part(11008, 1536)
        qpT = part(4608, 2048).rearrange("p (n t) -> p n t", n=2 * HEADS)
        s_all = part(6656, 2048)

        ms = sb("ms", [P, 16])
        rs = sb("rs", [P, 16])
        rt = sb("rt", [P, 16])
        hr = sb("hr", [P, 1])
        den = sb("den", [P, 4])
        nmx = sb("nmx", [P, 4])
        rp = sb("rp", [P, 4, NQH, HALF_ROT])
        sc = sb("sc", [P, 2, N_KEYS])
        sc2 = sb("sc2", [P, 2, N_KEYS])
        tv = sb("tv", [P, 2, TOPK])
        ti = sb("ti", [P, 2, TOPK], U32)
        tif = sb("tif", [P, 2, TOPK])
        cand = sb("cand", [P, TOPK, TOPK])
        cs = sb("cs", [P, TOPK])
        ci = sb("ci", [P, TOPK], U32)
        ab = sb("ab", [P, 2, TOPK], U32)
        abf = sb("abf", [P, 2, TOPK])
        hot = sb("hot", [P, 2 * TOPK, TOPK])
        ef = sb("ef", [P, 2, TOPK])
        en = sb("en", [P, TOPK])
        gsum = sb("gsum", [P, HEADS])
        idx_cur = sb("idx_cur", [P, TOPK], U32)
        z = sb("z", [P, TOPK])
        zi = sb("zi", [P, TOPK])
        ez = sb("ez", [P, TOPK])
        gz = sb("gz", [P, TOPK])
        act_w = sb("act_w", [P, TOPK])
        diag = sb("diag", [P, DIAGS, P])

        def pb(name, width):
            return ctx.enter_context(nc.psum_tensor(name, [P, width], F32))

        acc = pb("acc", D)
        bank = [pb("bank0", 512), pb("bank1", 512)]
        tr = pb("tr", D)
        scp = pb("scp", D)

        consts_in = sem("consts_in")
        late_in = sem("late_in")
        w_in = [sem(f"w_in{r}") for r in range(WRING)]
        w_used = sem("w_used")
        bank_read = sem("bank_read")
        u_in = [sem(f"u_in{r}") for r in range(RING)]
        v_in = [sem(f"v_in{r}") for r in range(RING)]
        u_used = sem("u_used")
        v_used = sem("v_used")
        pool_tick = sem("pool_tick")
        dve_tick = sem("dve_tick")
        idx_ready = sem("idx_ready")
        idx_set = sem("idx_set")
        zi_ready = sem("zi_ready")
        ez_ready = sem("ez_ready")
        act_ready = sem("act_ready")
        diag_ready = sem("diag_ready")
        acc_done = sem("acc_done")
        acc_read = sem("acc_read")
        dve_rows = sem("dve_rows")
        dve_side = sem("dve_side")
        act_side = sem("act_side")
        squares = sem("squares")
        roots = sem("roots")
        to_transpose = sem("to_transpose")
        transposed = sem("transposed")
        transposes_read = sem("transposes_read")
        argument = sem("argument")
        value = sem("value")
        projected = sem("projected")
        operands = sem("operands")
        pair_full = sem("pair_full")
        pair_read = sem("pair_read")
        state_full = sem("state_full")
        state_read = sem("state_read")
        probs_ready = sem("probs_ready")
        pv_done = sem("pv_done")
        scored = sem("scored")
        routed = sem("routed")
        stored = sem("stored")

        PHASE_OF = [(0, 0), (0, 1), (1, 0), (1, 1)]
        block = ctx.enter_context(nc.Block())

        def run(gather, side):
            for _ in side(0):
                pass
            for phase in range(PHASES):
                if phase + 1 == PHASES:
                    gather(phase, 0, HEADS)
                    break
                pieces = side(phase + 1)
                lo = 0
                for heads, count in zip(CUTS, PIECES):
                    gather(phase, lo, lo + heads)
                    lo += heads
                    for _ in range(count):
                        next(pieces, None)
                for _ in pieces:
                    pass

        @block.sync
        def _(sp):
            for dst, src in ((h[:, 0, :], x_d[0]), (h[:, 1, :], x_d[1]), (ident[:, :], ident_d),
                             (lbl[:, :, :], lb_d), (headg[:, :, :], headg_d), (rope[:, :, :, :], rope_d),
                             (on, lmask_d), (iota[:, :], iota_d), (skt[:, :, :, :], skt_d)):
                sp.dma_start(dst, src).then_inc(consts_in, 16)
            for n in range(4):
                sp.dma_start(gains[:, n, :], gains_d[n:n + 1, :].to_broadcast([P, D])).then_inc(consts_in, 16)
            sp.sem_inc(w_used, WRING)
            at = 0

            def stream(at, first, count):
                whole = count // WRING
                with sp.Fori(0, whole) as i:
                    for j in range(WRING):
                        sp.wait_ge(w_used, i * WRING + (at + j + 1))
                        sp.dma_start(w_ring[:, (at + j) % WRING, :],
                                     wall_d[bass.ds(i * WRING + (first + j), 1), :, :].rearrange("o p n -> p (o n)"))\
                          .then_inc(w_in[(at + j) % WRING], 16)
                for j in range(whole * WRING, count):
                    sp.wait_ge(w_used, at + j + 1)
                    sp.dma_start(w_ring[:, (at + j) % WRING, :], wall_d[first + j]).then_inc(w_in[(at + j) % WRING], 16)
                return at + count

            for t in range(TILES):
                at = stream(at, W_IN, W_KV - W_IN)
                at = stream(at, W_P0, W_P1 - W_P0)
            sp.wait_ge(routed, 2)
            sp.dma_start(amask, amask_d).then_inc(late_in, 16)
            sp.dma_start(gains[:, GAIN_F1, :], gains_d[GAINS - 1:GAINS, :].to_broadcast([P, D])).then_inc(late_in, 16)
            for t in range(TILES):
                at = stream(at, W_KV, W_P0 - W_KV)
                at = stream(at, W_P1, W_END - W_P1)
            for t in range(TILES):
                sp.wait_ge(acc_read, 2 + t + 1)
                sp.dma_start(out_d[t], h[:, t, :]).then_inc(stored, 16)
            sp.wait_ge(stored, 16 * TILES)

        @block.gpsimd
        def _(pool):
            pool.sem_inc(u_used, RING)
            pool.sem_inc(v_used, RING + 1)
            with pool.Fori(0, PHASES * HEADS) as i:
                pool.wait_ge(idx_ready, i + 1)
                for g in range(GROUPS):
                    pool.wait_ge(v_used, i * TOPK + (g * RING + 1))
                    nc.gpsimd.tensor_copy(idx_cur[:, g * RING:(g + 1) * RING],
                                          idx_all[:, bass.ds(i * TOPK + g * RING, RING)]).then_inc(idx_set, 1)
                    pool.wait_ge(idx_set, i * GROUPS + (g + 1))
                    for ring, table, arrived, used, credit in ((u_ring, u_d, u_in, u_used, 0),
                                                               (v_ring, v_d, v_in, v_used, 1)):
                        for r in range(RING):
                            pool.wait_ge(used, i * TOPK + (g * RING + r + 1 + credit))
                            pool.sem_inc(pool_tick, 1)
                            nc.gpsimd.indirect_dma_start(
                                out=ring[:, r, :], out_offset=None, in_=table,
                                in_offset=bass.IndirectOffsetOnAxis(ap=idx_cur[:, g * RING + r:g * RING + r + 1], axis=0))\
                                .then_inc(arrived[r], 16)

        @block.vector
        def _(dve):
            V = nc.vector
            chain = Chain(dve, dve_side)
            rows = Chain(dve, dve_rows)
            link, tick = chain.link, chain.tick
            count = Count()

            def tt(out, a, b, op):
                return V.tensor_tensor(out, a, b, op)

            def wait_next(sem, n=1):
                dve.wait_ge(sem, count.next(sem.name, n))

            def over(ap, n):
                return ap.unsqueeze(2).to_broadcast([P, ap.shape[1], n])

            def rsqrt(n):
                link(V.tensor_scalar(ms[:, 0:n], ms[:, 0:n], EPS, None, ALU.add))
                dve.sem_inc(squares, 1)
                wait_next(roots)
                link(tt(rt[:, 0:n], rs[:, 0:n], rs[:, 0:n], ALU.mult))
                link(tt(rt[:, 0:n], rt[:, 0:n], ms[:, 0:n], ALU.mult))
                link(V.tensor_scalar(rt[:, 0:n], rt[:, 0:n], -0.5, 1.5, ALU.mult, ALU.add))
                link(tt(rs[:, 0:n], rs[:, 0:n], rt[:, 0:n], ALU.mult))

            def token_rsqrt(t):
                link(V.scalar_tensor_tensor(out=xn[:, :], in0=h[:, t, :], scalar=1.0, in1=h[:, t, :],
                                            op0=ALU.mult, op1=ALU.mult, accum_out=ms[:, 0:1]))
                link(V.tensor_scalar(ms[:, 0:1], ms[:, 0:1], 1.0 / D, None, ALU.mult))
                rsqrt(1)

            def head_rsqrt(src, n):
                link(V.tensor_reduce(ms[:, 0:n], src.rearrange("p (n e) -> p n e", n=n), AX.X, ALU.add))
                link(V.tensor_scalar(ms[:, 0:n], ms[:, 0:n], 1.0 / HD, None, ALU.mult))
                rsqrt(n)

            def scale_gain(t, gain, dst, scale):
                link(V.scalar_tensor_tensor(out=dst, in0=h[:, t, :], scalar=scale, in1=gains[:, gain, :],
                                            op0=ALU.mult, op1=ALU.mult))
                count.transposes += 1
                dve.sem_inc(to_transpose, 1)

            def ask():
                dve.sem_inc(argument, 1)

            def answer():
                wait_next(value)

            def from_pe():
                wait_next(pair_full)

            def pair_is_read():
                dve.sem_inc(pair_read, 1)

            def sigmoid_of_exp(e):
                link(V.tensor_scalar(e, e, 1.0, None, ALU.add))
                link(V.reciprocal(e, e))

            def add_residual(t, chunks):
                for c in range(2):
                    count.chunks += chunks
                    dve.wait_ge(w_used, WRING + count.chunks)
                    hc = h[:, t, c * 512:(c + 1) * 512]
                    link(tt(hc, hc, bank[count.banks % 2][:, :], ALU.add))
                    dve.sem_inc(bank_read, 1)
                    count.banks += 1

            def heads_of(a, n=HG_HEADS):
                return a.rearrange("p (n e) -> p n e", n=n)

            def hgrn(t):
                token_rsqrt(t)
                scale_gain(t, GAIN_HG, xn[:, :], rs[:, 0:1])
                yield
                wait_next(projected)
                sigmoid_of_exp(eT)
                link(tt(qT, qT, eT, ALU.mult))
                yield
                wait_next(projected)
                sigmoid_of_exp(raw)
                link(tt(heads_of(raw), heads_of(raw), over(lb1[:, :], P), ALU.mult))
                link(tt(heads_of(raw), heads_of(raw), over(lb[:, :], P), ALU.add))
                ask()
                link(V.tensor_scalar(kT, raw, -1.0, 1.0, ALU.mult, ALU.add))
                dve.sem_inc(operands, 1)
                link(V.memset(sT, 0.0))
                answer()
                for n in range(HG_HEADS):
                    c = slice(n * P, (n + 1) * P)
                    (link if n == HG_HEADS - 1 else tick)(
                        V.tensor_tensor_scan(bT[:, c], ones[:, :], eT[:, c], 0.0, ALU.mult, ALU.add))
                tick(V.tensor_copy(qe, qT))
                link(V.tensor_copy(ke, kT))
                yield
                wait_next(projected)
                sigmoid_of_exp(on)
                link(tt(gi, gi, on, ALU.mult))

                def exponents(level):
                    w = P >> level
                    b4, e4 = (a.rearrange("p (n s w) -> p n s w", s=2, w=w) for a in (bT, eT))
                    ref = b4[:, :, 0, w - 1:w].to_broadcast([P, D // (2 * w), w])
                    tick(tt(e4[:, :, 1, :], b4[:, :, 1, :], ref, ALU.subtract))
                    link(tt(e4[:, :, 0, :], ref, b4[:, :, 0, :], ALU.subtract))
                    ask()

                def half(a, level, s):
                    return a.rearrange("p (n s w) -> p n s w", s=2, w=P >> level)[:, :, s, :]

                exponents(1)
                for level in range(LEVELS + 1):
                    from_pe()
                    pair = (scp, tr)[count.pairs % 2]
                    count.pairs += 1
                    link(V.copy_predicated(heads_of(sT), lmask[:, level:level + 1, :].to_broadcast([P, HG_HEADS, P]),
                                           heads_of(pair[:, :])))
                    pair_is_read()
                    if level < LEVELS:
                        answer()
                        tick(tt(half(qe, level + 1, 1), half(qT, level + 1, 1), half(eT, level + 1, 1), ALU.mult))
                        link(tt(half(ke, level + 1, 0), half(kT, level + 1, 0), half(eT, level + 1, 0), ALU.mult))
                        dve.sem_inc(operands, 1)
                        if level + 2 <= LEVELS:
                            exponents(level + 2)
                    if level == 3:
                        yield
                if t > 0:
                    ask()
                    answer()
                    link(tt(qe, qT, eT, ALU.mult))
                dve.sem_inc(operands, 1)
                yield
                from_pe()
                answer()
                head_rsqrt(eT, HG_HEADS)
                link(tt(heads_of(on), heads_of(scp[:, :]), over(rs[:, 0:HG_HEADS], HD), ALU.mult))
                pair_is_read()
                count.pairs += 1
                link(tt(heads_of(on), heads_of(on), headg[:, 0:1, :].to_broadcast([P, HG_HEADS, HD]), ALU.mult))
                link(tt(on, on, gi, ALU.mult))
                dve.sem_inc(to_transpose, 1)
                count.transposes += 1
                if t == 0:
                    b3 = heads_of(bT)
                    link(tt(heads_of(eT), b3[:, :, P - 1:P].to_broadcast([P, HG_HEADS, P]), b3, ALU.subtract))
                    ask()
                    answer()
                    link(tt(ke, kT, eT, ALU.mult))
                    dve.sem_inc(to_transpose, 1)
                    count.transposes += 1
                count.chunks += 16
                count.banks += 8
                add_residual(t, 2)

            def rotate(x, n, t):
                x3 = heads_of(x, n)
                x1, x2 = x3[:, :, 0:HALF_ROT], x3[:, :, HALF_ROT:2 * HALF_ROT]
                cos, sin = (rope[:, t, m:m + 1, :].to_broadcast([P, n, HALF_ROT]) for m in range(2))
                tick(tt(rp[:, 0, 0:n, :], x1, cos, ALU.mult))
                tick(tt(rp[:, 1, 0:n, :], x2, sin, ALU.mult))
                tick(tt(rp[:, 2, 0:n, :], x2, cos, ALU.mult))
                link(tt(rp[:, 3, 0:n, :], x1, sin, ALU.mult))
                tick(tt(x1, rp[:, 0, 0:n, :], rp[:, 1, 0:n, :], ALU.subtract))
                link(tt(x2, rp[:, 2, 0:n, :], rp[:, 3, 0:n, :], ALU.add))

            def norm_heads(x, n, gain):
                link(tt(sq[:, 0:n * HD], x, x, ALU.mult))
                head_rsqrt(sq[:, 0:n * HD], n)
                link(tt(heads_of(x, n), heads_of(x, n), over(rs[:, 0:n], HD), ALU.mult))
                link(tt(heads_of(x, n), heads_of(x, n), headg[:, gain:gain + 1, :].to_broadcast([P, n, HD]), ALU.mult))

            def attention(t):
                token_rsqrt(t)
                link(V.tensor_copy(hr[:, :], rs[:, 0:1]))
                scale_gain(t, GAIN_KV, xn[:, :], hr[:, :])
                dve.wait_ge(transposed, count.transposes)
                scale_gain(t, GAIN_ATT, xn[:, :], hr[:, :])
                yield
                wait_next(projected)
                norm_heads(ks, NKH, 1)
                rotate(ks, NKH, t)
                dve.sem_inc(to_transpose, 1)
                yield
                wait_next(projected)
                norm_heads(qs, NQH, 2)
                rotate(qs, NQH, t)
                dve.sem_inc(to_transpose, 1)
                count.transposes += 3
                yield
                nk = P * (t + 1)
                mask = amask[:, 0:3 * P] if t == 0 else amask[:, 3 * P:9 * P]
                o = bank[(count.banks + 6) % 2]
                dve.wait_ge(late_in, 32)
                for j in range(NJH):
                    from_pe()
                    count.pairs += 1
                    link(V.scalar_tensor_tensor(out=pr[:, 0:3 * nk], in0=scp[:, 0:3 * nk], scalar=HD ** -0.5, in1=mask,
                                                op0=ALU.mult, op1=ALU.add))
                    pair_is_read()
                    link(V.tensor_reduce(nmx[:, j:j + 1], pr[:, 0:3 * nk], AX.X, ALU.max, negate=True))
                    ask()
                    wait_next(pv_done)
                    link(V.reciprocal(rt[:, j:j + 1], den[:, j:j + 1]))
                    link(V.tensor_scalar(oat[:, j * HD:(j + 1) * HD], o[:, j * HD:(j + 1) * HD], rt[:, j:j + 1], None,
                                         ALU.mult))
                count.transposes += NJH + 1
                dve.sem_inc(bank_read, 1)
                dve.sem_inc(to_transpose, 1)
                yield
                count.chunks += 12
                count.banks += 7
                add_residual(t, 1)

            def apart(ins):
                chain.link_apart(ins, dve_tick)

            def route(phase):
                layer, t = PHASE_OF[phase]
                token_rsqrt(t)
                scale_gain(t, (GAIN_F0, GAIN_F1)[layer], xp[:, t, :], rs[:, 0:1])
                yield
                count.chunks += 8
                count.banks += 8
                yield
                wait_next(projected)
                for part_of in range(4):
                    first = part_of * HEADS // 4
                    with dve.Fori(0, HEADS // 4) as i:
                        chain.enter(i, ROUTE_LINKS)
                        apart(V.tensor_copy(sc[:, :, :].rearrange("p a n -> p (a n)"),
                                           s_all[:, bass.ds(i * 2 * N_KEYS + first * 2 * N_KEYS, 2 * N_KEYS)]))
                        for a in range(2):
                            (apart if a else tick)(V.max(tv[:, a, 0:8], sc[:, a, :]))
                        for a in range(2):
                            tick(V.max_index(ti[:, a, 0:8], tv[:, a, 0:8], sc[:, a, :]))
                            (apart if a else tick)(V.match_replace(sc2[:, a, :], tv[:, a, 0:8], sc[:, a, :], LOWEST))
                        for a in range(2):
                            (apart if a else tick)(V.max(tv[:, a, 8:16], sc2[:, a, :]))
                        for a in range(2):
                            tick(V.max_index(ti[:, a, 8:16], tv[:, a, 8:16], sc2[:, a, :]))
                        apart(tt(cand[:, :, :], over(tv[:, 0, :], TOPK), tv[:, 1:2, :].to_broadcast([P, TOPK, TOPK]),
                                ALU.add))
                        tick(V.tensor_copy(tif[:, :, :], ti[:, :, :]))
                        c = cand[:, :, :].rearrange("p a b -> p (a b)")
                        apart(V.max(cs[:, 0:8], c))
                        tick(V.max_index(ci[:, 0:8], cs[:, 0:8], c))
                        apart(V.match_replace(c, cs[:, 0:8], c, LOWEST))
                        apart(V.max(cs[:, 8:16], c))
                        link(V.max_index(ci[:, 8:16], cs[:, 8:16], c))
                        tick(V.tensor_scalar(ab[:, 0, :], ci[:, :], 4, None, ALU.logical_shift_right))
                        link(V.tensor_scalar(ab[:, 1, :], ci[:, :], TOPK - 1, None, ALU.bitwise_and))
                        link(V.tensor_copy(abf[:, :, :], ab[:, :, :]))
                        link(tt(hot[:, :, :], over(abf[:, :, :].rearrange("p a k -> p (a k)"), TOPK),
                                iota[:, :].unsqueeze(1).to_broadcast([P, 2 * TOPK, TOPK]), ALU.is_equal))
                        h4 = hot[:, :, :].rearrange("p (a k) n -> p a k n", a=2)
                        link(tt(h4, h4, tif[:, :, :].unsqueeze(2).to_broadcast([P, 2, TOPK, TOPK]), ALU.mult))
                        link(V.tensor_reduce(ef[:, :, :].rearrange("p a k -> p (a k)"), hot[:, :, :], AX.X, ALU.add))
                        link(V.scalar_tensor_tensor(out=en[:, :], in0=ef[:, 0, :], scalar=float(N_KEYS), in1=ef[:, 1, :],
                                                    op0=ALU.mult, op1=ALU.add))
                        V.tensor_scalar(idx_all[:, bass.ds(i * TOPK + (phase * SLOTS + first * TOPK), TOPK)], en[:, :],
                                        float(layer * N_EXPERTS), None, ALU.add).then_inc(idx_ready, 1)
                        link(V.tensor_scalar(gate_all[:, bass.ds(i * TOPK + (phase * SLOTS + first * TOPK), TOPK)],
                                             cs[:, :], cs[:, 0:1], None, ALU.subtract))
                    chain.leave(HEADS // 4)
                    if part_of < 3:
                        yield
                ask()
                answer()
                g3 = gate_all[:, phase * SLOTS:(phase + 1) * SLOTS].rearrange("p (n k) -> p n k", n=HEADS)
                link(V.tensor_reduce(gsum[:, :], g3, AX.X, ALU.add))
                link(V.reciprocal(gsum[:, :], gsum[:, :]))
                link(tt(g3, g3, over(gsum[:, :], TOPK), ALU.mult))
                dve.sem_inc(routed, 1)

            def side(phase):
                layer, t = PHASE_OF[phase]
                yield from (attention if layer else hgrn)(t)
                yield from route(phase)

            def gather(phase, lo, hi):
                layer, t = PHASE_OF[phase]
                first = phase * HEADS + lo
                with dve.Fori(0, hi - lo) as i:
                    rows.enter(i, ROW_LINKS * GROUPS)
                    for g in range(GROUPS):
                        c = slice(g * RING, (g + 1) * RING)
                        for r in range(RING):
                            dve.wait_ge(u_in[r], i * (16 * GROUPS) + 16 * (first * GROUPS + g + 1))
                            V.scalar_tensor_tensor(out=u_ring[:, r, :], in0=u_ring[:, r, :], scalar=1.0, in1=xp[:, t, :],
                                                   op0=ALU.mult, op1=ALU.mult,
                                                   accum_out=z[:, g * RING + r:g * RING + r + 1]).then_inc(u_used, 1)
                        dve.wait_ge(u_used, i * TOPK + (first * TOPK + (g + 1) * RING + RING))
                        rows.tick(V.tensor_copy(gz[:, c], gate_all[:, bass.ds(i * TOPK + (first * TOPK + g * RING), RING)]))
                        rows.link(tt(zi[:, c], z[:, c], z[:, c], ALU.mult))
                        rows.link(V.tensor_scalar(zi[:, c], zi[:, c], GELU_CUBE, 1.0, ALU.mult, ALU.add))
                        tt(zi[:, c], zi[:, c], z[:, c], ALU.mult).then_inc(zi_ready, 1)
                        rows.link(tt(gz[:, c], gz[:, c], z[:, c], ALU.mult))
                        dve.wait_ge(ez_ready, i * GROUPS + (first * GROUPS + g + 1))
                        rows.link(V.tensor_scalar(ez[:, c], ez[:, c], 1.0, None, ALU.add))
                        rows.link(V.reciprocal(ez[:, c], ez[:, c]))
                        tt(act_w[:, c], ez[:, c], gz[:, c], ALU.mult).then_inc(act_ready, 1)
                rows.leave(hi - lo)
                if hi == HEADS:
                    dve.wait_ge(acc_done, phase + 1)
                    tick(V.tensor_copy(h[:, t, 0:512], acc[:, 0:512]))
                    link(V.tensor_copy(h[:, t, 512:D], acc[:, 512:D]))
                    dve.sem_inc(acc_read, 1)

            link(V.memset(zero[:, :], 0.0))
            link(V.memset(ones[:, :], 1.0))
            dve.wait_ge(consts_in, 16 * CONSTS)
            link(V.tensor_copy(lmask[:, :, :].rearrange("p l t -> p (l t)"), on))
            link(tt(lb1[:, :], lbl[:, 0, :], lbl[:, 1, :], ALU.max))
            link(tt(lbl[:, :, :], lbl[:, :, :], lb1[:, :].unsqueeze(1).to_broadcast([P, 2, HG_HEADS]), ALU.subtract))
            ask()
            answer()
            link(tt(lb1[:, :], lbl[:, 0, :], lbl[:, 1, :], ALU.add))
            link(V.reciprocal(lb1[:, :], lb1[:, :]))
            link(tt(lb[:, :], lbl[:, 0, :], lb1[:, :], ALU.mult))
            link(V.tensor_scalar(lb1[:, :], lb[:, :], -1.0, 1.0, ALU.mult, ALU.add))
            run(gather, side)

        @block.scalar
        def _(act):
            A = nc.scalar
            chain = Chain(act, act_side)
            link, tick = chain.link, chain.tick
            count = Count()

            def wait_next(sem, n=1):
                act.wait_ge(sem, count.next(sem.name, n))

            def give_roots(n):
                wait_next(squares)
                link(A.activation(rs[:, 0:n], ms[:, 0:n], ACT.Ln))
                link(A.activation(rs[:, 0:n], rs[:, 0:n], ACT.Exp, scale=-0.5))
                act.sem_inc(roots, 1)

            def give(out, in_, func, **more):
                wait_next(argument)
                link(A.activation(out, in_, func, **more))
                act.sem_inc(value, 1)

            def take_transposes(*copies):
                count.transposes += 1
                act.wait_ge(transposed, count.transposes)
                for n, (dst, src) in enumerate(copies):
                    (link if n == len(copies) - 1 else tick)(A.activation(dst, src, ACT.Copy))
                act.sem_inc(transposes_read, 1)

            def take_width(dst):
                take_transposes(*((dst[:, 4 * c:4 * c + 4, :].rearrange("p n t -> p (n t)"), tr[:, c * 512:(c + 1) * 512])
                                  for c in range(2)))

            def take_bank(chunks, *moves):
                count.chunks += chunks
                act.wait_ge(w_used, WRING + count.chunks)
                source = bank[count.banks % 2]
                for n, (dst, first, width, func, scale) in enumerate(moves):
                    (link if n == len(moves) - 1 else tick)(
                        A.activation(dst, source[:, first:first + width], func, scale=scale))
                act.sem_inc(bank_read, 1)
                count.banks += 1

            def hgrn(t):
                give_roots(1)
                take_width(xT)
                for c in range(2):
                    s = slice(c * 512, (c + 1) * 512)
                    take_bank(2, (qT[:, s], 0, 512, ACT.Copy, 1.0), (eT[:, s], 0, 512, ACT.Exp, -1.0))
                act.sem_inc(projected, 1)
                yield
                for c in range(2):
                    take_bank(2, (raw[:, c * 512:(c + 1) * 512], 0, 512, ACT.Exp, -1.0))
                act.sem_inc(projected, 1)
                yield
                give(eT, raw, ACT.Ln)
                for c in range(2):
                    take_bank(2, (vi[:, c * 512:(c + 1) * 512], 0, 512, ACT.Copy, 1.0))
                yield
                for c in range(2):
                    s = slice(c * 512, (c + 1) * 512)
                    take_bank(2, (gi[:, s], 0, 512, ACT.Copy, 1.0), (on[:, s], 0, 512, ACT.Exp, -1.0))
                act.sem_inc(projected, 1)
                for level in range(1, LEVELS + 1):
                    give(eT, eT, ACT.Exp)
                    if level == 5:
                        yield
                if t > 0:
                    give(eT, bT, ACT.Exp)
                yield
                act.wait_ge(pair_full, count.next(pair_full.name, LEVELS + 2))
                link(A.activation(eT, scp[:, :], ACT.Square))
                act.sem_inc(value, 1)
                give_roots(HG_HEADS)
                take_width(xT)
                if t == 0:
                    give(eT, eT, ACT.Exp)
                    take_width(qe.rearrange("p (n t) -> p n t", n=HG_HEADS))
                    wait_next(state_full)
                    link(A.activation(state, scp[:, :], ACT.Copy))
                    act.sem_inc(state_read, 1)
                count.chunks += 4
                count.banks += 2

            def attention(t):
                give_roots(1)
                take_width(xT)
                take_bank(2, (ks[:, 0:512], 0, 512, ACT.Copy, 1.0))
                take_bank(2, (ks[:, 512:768], 0, 256, ACT.Copy, 1.0), (val[:, t, 0:256], 256, 256, ACT.Copy, 1.0))
                take_bank(2, (val[:, t, 256:768], 0, 512, ACT.Copy, 1.0))
                act.sem_inc(projected, 1)
                take_width(xT)
                yield
                for c in range(3):
                    take_bank(2, (qs[:, c * 512:(c + 1) * 512], 0, 512, ACT.Copy, 1.0))
                act.sem_inc(projected, 1)
                give_roots(NKH)
                yield
                tokens = slice(t * P, (t + 1) * P)
                t3 = tr[:, :].rearrange("p (n t) -> p n t", n=KT_D)
                take_transposes((keyT[:, 0:4, tokens], t3[:, 0:4, :]), (keyT[:, 4:6, tokens], t3[:, 4:6, :]))
                give_roots(NQH)
                yield
                take_width(qhT[:, 0:8, :])
                take_transposes((qhT[:, 8:12, :].rearrange("p n t -> p (n t)"), tr[:, 0:512]))
                nk = P * (t + 1)
                nb = 3 * (t + 1)
                for j in range(NJH):
                    wait_next(argument)
                    link(A.activation(pr[:, 0:3 * nk], pr[:, 0:3 * nk], ACT.Exp, bias=nmx[:, j:j + 1],
                                      accum_out=den[:, j:j + 1]))
                    act.sem_inc(probs_ready, 1)
                    blocks = [(0, min(4, nb))] + ([(4, nb)] if nb > 4 else [])
                    take_transposes(*((prT[:, a:b, :].rearrange("p n t -> p (n t)"), tr[:, a * P:b * P]) for a, b in blocks))
                count.banks += 1
                yield
                take_transposes((xT[:, 0:4, :].rearrange("p n t -> p (n t)"), tr[:, 0:512]))
                count.chunks += 2
                count.banks += 2

            def route(phase):
                give_roots(1)
                take_width(xT)
                yield
                for c in range(4):
                    take_bank(2, (qpT[:, 4 * c:4 * c + 4, :].rearrange("p n t -> p (n t)"), 0, 512, ACT.Copy, 1.0))
                for c in range(4):
                    wait_next(scored)
                    link(A.activation(s_all[:, c * 512:(c + 1) * 512], bank[count.banks % 2][:, :], ACT.Copy))
                    act.sem_inc(bank_read, 1)
                    count.banks += 1
                act.sem_inc(projected, 1)
                yield
                yield
                yield
                yield
                g = gate_all[:, phase * SLOTS:(phase + 1) * SLOTS]
                give(g, g, ACT.Exp)

            def side(phase):
                layer, t = PHASE_OF[phase]
                yield from (attention if layer else hgrn)(t)
                yield from route(phase)

            def gather(phase, lo, hi):
                first = phase * HEADS + lo
                with act.Fori(0, hi - lo) as i:
                    for g in range(GROUPS):
                        c = slice(g * RING, (g + 1) * RING)
                        act.wait_ge(zi_ready, i * GROUPS + (first * GROUPS + g + 1))
                        A.activation(ez[:, c], zi[:, c], ACT.Exp, scale=-GELU_SCALE).then_inc(ez_ready, 1)
                        act.wait_ge(act_ready, i * GROUPS + (first * GROUPS + g + 1))
                        for r in range(RING):
                            act.wait_ge(v_used, i * TOPK + (first * TOPK + g * RING + r + 2 + RING - DIAGS))
                            A.activation(diag[:, r % DIAGS, :], ident[:, :], ACT.Copy,
                                         scale=act_w[:, g * RING + r:g * RING + r + 1]).then_inc(diag_ready, 1)

            act.wait_ge(consts_in, 16 * CONSTS)
            give(lbl[:, :, :], lbl[:, :, :], ACT.Exp)
            run(gather, side)

        @block.tensor
        def _(pe):
            M = nc.tensor.matmul
            count = Count()

            def wait_next(sem, n=1):
                pe.wait_ge(sem, count.next(sem.name, n))

            def transpose(blocks):
                if count.transposes:
                    pe.wait_ge(transposes_read, count.transposes)
                if count.pairs:
                    pe.wait_ge(pair_read, count.pairs)
                for n, src in enumerate(blocks):
                    ins = nc.tensor.transpose(tr[:, n * P:(n + 1) * P], src, ident[:, :])
                ins.then_inc(transposed, 1)
                count.transposes += 1

            def transpose_new(blocks):
                wait_next(to_transpose)
                transpose(blocks)

            def width(a):
                return [a[:, n * P:(n + 1) * P] for n in range(KT_D)]

            def take_turn():
                if count.banks >= 2:
                    pe.wait_ge(bank_read, count.banks - 1)
                count.banks += 1
                return bank[(count.banks - 1) % 2]

            def next_chunk():
                n = count.chunks
                count.chunks += 1
                pe.wait_ge(w_in[n % WRING], 16 * (n // WRING + 1))
                return w_ring[:, n % WRING, :]

            def project(turns, across):
                pe.wait_ge(transposes_read, count.transposes)
                for _ in range(turns):
                    out = take_turn()
                    for c in range(2):
                        w = next_chunk().rearrange("p (k n) -> p k n", k=KT_D)
                        if across:
                            for b in range(2):
                                for k in range(KT_D):
                                    ins = M(out[:, (2 * c + b) * P:(2 * c + b + 1) * P], w[:, k, b * P:(b + 1) * P],
                                            xT[:, k, :], start=k == 0, stop=k == KT_D - 1)
                        else:
                            for k in range(KT_D):
                                ins = M(out[:, c * 256:(c + 1) * 256], xT[:, k, :], w[:, k, :], start=k == 0,
                                        stop=k == KT_D - 1)
                        ins.then_inc(w_used, 1)

            def hgrn(t):
                transpose_new(width(xn))
                project(2, True)
                yield
                project(2, True)
                yield
                project(2, False)
                yield
                project(2, False)
                if t > 0:
                    pe.wait_ge(state_read, 1)
                for level in range(LEVELS + 1):
                    wait_next(operands)
                    if count.pairs >= 2:
                        pe.wait_ge(pair_read, count.pairs - 1)
                    pair = (scp, tr)[count.pairs % 2]
                    count.pairs += 1
                    a, b = (ke, qe) if level else (kT, qT)
                    for n in range(HG_HEADS):
                        s = slice(n * P, (n + 1) * P)
                        ins = M(pair[:, s], a[:, s], b[:, s], start=True, stop=True)
                    ins.then_inc(pair_full, 1)
                    if level == 3:
                        yield
                wait_next(operands)
                pe.wait_ge(pair_read, count.pairs)
                wait_next(projected, 3)
                for n in range(HG_HEADS):
                    s = slice(n * P, (n + 1) * P)
                    ins = M(scp[:, s], sT[:, s], vi[:, s], start=True, stop=t == 0)
                    if t > 0:
                        ins = M(scp[:, s], qe[:, s], state[:, s], start=False, stop=True)
                ins.then_inc(pair_full, 1)
                count.pairs += 1
                yield
                transpose_new(width(on))
                if t == 0:
                    transpose_new(width(ke))
                    pe.wait_ge(transposes_read, count.transposes)
                    for n in range(HG_HEADS):
                        s = slice(n * P, (n + 1) * P)
                        ins = M(scp[:, s], qe[:, s], vi[:, s], start=True, stop=True)
                    ins.then_inc(state_full, 1)
                project(2, False)

            def attention(t):
                transpose_new(width(xn))
                project(3, False)
                transpose_new(width(xn))
                yield
                project(3, False)
                yield
                transpose_new([ks[:, n * HD:(n + 1) * HD] for n in range(NKH)])
                yield
                transpose_new([qs[:, n * HD:(n + 1) * HD] for n in range(8)])
                transpose([qs[:, n * HD:(n + 1) * HD] for n in range(8, NQH)])
                pe.wait_ge(transposes_read, count.transposes)
                nk = P * (t + 1)
                o = take_turn()

                def score(j):
                    pe.wait_ge(pair_read, count.pairs)
                    for g in range(N_GROUPS):
                        ins = M(scp[:, g * nk:(g + 1) * nk], qhT[:, g * NJH + j, :],
                                keyT[:, g * KV_PER_GROUP + j // Q_PER_KV, 0:nk], start=True, stop=True)
                    ins.then_inc(pair_full, 1)
                    count.pairs += 1

                score(0)
                for j in range(NJH):
                    if j + 1 < NJH:
                        score(j + 1)
                    wait_next(probs_ready)
                    transpose_probs([pr[:, n * P:(n + 1) * P] for n in range(3 * (t + 1))])
                    pe.wait_ge(transposes_read, count.transposes)
                    for n in range(3 * (t + 1)):
                        g, b = divmod(n, t + 1)
                        kv = g * KV_PER_GROUP + j // Q_PER_KV
                        ins = M(o[:, j * HD:(j + 1) * HD], prT[:, n, :], val[:, b, kv * HD:(kv + 1) * HD],
                                start=n == 0, stop=n == 3 * (t + 1) - 1)
                    ins.then_inc(pv_done, 1)
                yield
                transpose_new([oat[:, n * HD:(n + 1) * HD] for n in range(NJH)])
                pe.wait_ge(transposes_read, count.transposes)
                for c in range(2):
                    out = take_turn()
                    w = next_chunk().rearrange("p (k n) -> p k n", k=4)
                    for k in range(4):
                        ins = M(out[:, :], xT[:, k, :], w[:, k, :], start=k == 0, stop=k == 3)
                    ins.then_inc(w_used, 1)

            def transpose_probs(blocks):
                pe.wait_ge(transposes_read, count.transposes)
                for n, src in enumerate(blocks):
                    ins = nc.tensor.transpose(tr[:, n * P:(n + 1) * P], src, ident[:, :])
                ins.then_inc(transposed, 1)
                count.transposes += 1

            def route(phase):
                layer, t = PHASE_OF[phase]
                transpose_new([xp[:, t, n * P:(n + 1) * P] for n in range(KT_D)])
                yield
                project(4, True)
                for c in range(4):
                    out = take_turn()
                    pe.wait_ge(bank_read, count.banks - 4)
                    for b in range(4):
                        ins = M(out[:, b * P:(b + 1) * P], qpT[:, 4 * c + b, :], skt[:, layer, b % 2, :], start=True,
                                stop=True)
                    ins.then_inc(scored, 1)
                yield
                yield
                yield
                yield
                count.next(projected.name)

            def side(phase):
                layer, t = PHASE_OF[phase]
                yield from (attention if layer else hgrn)(t)
                yield from route(phase)

            def gather(phase, lo, hi):
                layer, t = PHASE_OF[phase]
                first = phase * HEADS + lo
                halves = [slice(0, 512), slice(512, D)]
                if lo == 0:
                    pe.wait_ge(routed, phase + 1)
                    if phase:
                        pe.wait_ge(acc_read, phase)
                    for s in halves:
                        M(acc[:, s], ident[:, :], h[:, t, s], start=True, stop=False)
                with pe.Fori(0, hi - lo) as i:
                    for g in range(GROUPS):
                        for r in range(RING):
                            pe.wait_ge(diag_ready, i * TOPK + (first * TOPK + g * RING + r + 1))
                            pe.wait_ge(v_in[r], i * (16 * GROUPS) + 16 * (first * GROUPS + g + 1))
                            for s in halves:
                                ins = M(acc[:, s], diag[:, r % DIAGS, :], v_ring[:, r, s], start=False, stop=False)
                            ins.then_inc(v_used, 1)
                if hi == HEADS:
                    for s in halves:
                        ins = M(acc[:, s].rearrange("p (n c) -> p n c", n=4), zero[:, :],
                                ident[:, :].unsqueeze(1).to_broadcast([P, 4, P]), start=False, stop=True)
                    ins.then_inc(acc_done, 1)

            pe.wait_ge(consts_in, 16 * CONSTS)
            run(gather, side)




def kernel(**inputs):
    import numpy as np
    import concourse.bacc as bacc
    from concourse import mybir as mb
    from concourse.bass_utils import run_bass_kernel_spmd

    get = {k: np.asarray(a) for k, a in inputs.items()}

    def chunks(w, rows):
        k, n = rows // P, CHUNK // (rows // P)
        return w.reshape(k, P, w.shape[1] // n, n).transpose(2, 1, 0, 3).reshape(-1, P, CHUNK)

    pq = get["peer_w_q"]
    wall = np.concatenate([chunks(get["hgrn_w_in"][0], D), chunks(get["hgrn_w_out"][0], D), chunks(get["w_kv"], D),
                           chunks(get["w_q"][0], D), chunks(get["w_o"][0], 512), chunks(pq[0], D), chunks(pq[1], D)])
    gains = np.stack([get["hgrn_norm"][0], get["kv_norm"], get["attn_norm"][0], get["ffn_norm"][0], get["ffn_norm"][1]])
    headg = np.ascontiguousarray(np.broadcast_to(
        np.stack([get["hgrn_out_norm"][0], get["k_norm"], get["q_norm"][0]])[None], (P, 3, HD)))
    lbl = get["hgrn_lb_logits"].reshape(2, HG_HEADS, P).transpose(2, 0, 1)
    skt = get["peer_sub_keys"].transpose(3, 0, 1, 2)

    tokens = TILES * P
    inv = np.float32(500000.0) ** (-np.arange(HALF_ROT, dtype=np.float32) * np.float32(2.0) / np.float32(2 * HALF_ROT))
    ang = np.arange(tokens, dtype=np.float32)[:, None] * inv[None, :].astype(np.float32)
    rope = np.stack([np.cos(ang), np.sin(ang)], 1).astype(np.float32).reshape(TILES, P, 2, HALF_ROT).transpose(1, 0, 2, 3)
    masks = []
    for t in range(TILES):
        i, j = np.arange(P)[:, None] + t * P, np.arange((t + 1) * P)[None, :]
        for window, step in ((128, 1), (512, 4), (2048, 16)):
            ok = (i >= j) & ((i - j) % step == 0) & (i - j <= window)
            masks.append(np.where(ok, 0.0, -1.0e30).astype(np.float32))
    amask = np.concatenate(masks, 1)
    j, i = np.arange(P)[:, None], np.arange(P)[None, :]
    level_masks = [i == j]
    for level in range(1, LEVELS + 1):
        w = P >> level
        level_masks.append((i // (2 * w) == j // (2 * w)) & ((i // w) % 2 == 1) & ((j // w) % 2 == 0))
    lmask = np.stack(level_masks, 1).astype(np.float32).reshape(P, -1)
    iota = np.ascontiguousarray(np.broadcast_to(np.arange(TOPK, dtype=np.float32), (P, TOPK)))

    nc = bacc.Bacc("TRN2", target_bir_lowering=False, num_devices=1)
    arrays, args = {}, []
    for name, a in dict(
            x=get["x"].reshape(TILES, P, D), wall=wall, gains=gains, lb=lbl, headg=headg, rope=rope, amask=amask,
            lmask=lmask, ident=np.eye(P, dtype=np.float32), iota=iota, skt=skt,
            u=get["peer_u"].reshape(-1, D), v=get["peer_v"].reshape(-1, D)).items():
        a = np.ascontiguousarray(a)
        arrays[f"in_{name}"] = a
        args.append(nc.dram_tensor(f"in_{name}", a.shape, mb.dt.from_np(a.dtype), kind="ExternalInput").ap())
    args.append(nc.dram_tensor("out_0", (TILES, P, D), mb.dt.float32, kind="ExternalOutput").ap())
    build(nc, *args)
    r = run_bass_kernel_spmd(nc, [arrays], core_ids=[0])
    return r.results[0]["out_0"].reshape(1, TILES * P, D)
```

```python
import concourse.bass as bass
from concourse import mybir
from contextlib import ExitStack

F32 = mybir.dt.float32
U32 = mybir.dt.uint32
U8 = mybir.dt.uint8
ALU = mybir.AluOpType
ACT = mybir.ActivationFunctionType
AX = mybir.AxisListType

P = 128
D = 1024
KT_D = D // P
TILES = 2
EPS = 1e-6
HG_HEADS = D // P
LEVELS = 7
HD = 128
N_GROUPS, KV_PER_GROUP, Q_PER_KV = 3, 2, 2
NQH = N_GROUPS * KV_PER_GROUP * Q_PER_KV
NKH = N_GROUPS * KV_PER_GROUP
NJH = KV_PER_GROUP * Q_PER_KV
HALF_ROT = HD // 8
HEADS = 8
TOPK = 16
PART = 2
N_KEYS = 128
N_EXPERTS = N_KEYS * N_KEYS
PHASES = 4
RING = 8
GROUPS = TOPK // RING
ROUNDS = HEADS * GROUPS
SLOTS = HEADS * TOPK
WRING = 4
CHUNK = 2048
GELU_CUBE = 0.044715
GELU_SCALE = 0.7978845608028654
LOWEST = -3.0e38
EARLY, LATER, LATE = 4, 7, 3
ROW_LINKS = 4
RSQRT_SEED = float(0x5F3759DF)

W_IN, W_OUT, W_KV, W_Q, W_O, W_P0, W_P1, W_END = 0, 16, 20, 26, 32, 34, 42, 50
GAIN_ROWS = 5
ROW_HG, ROW_KV, ROW_ATT, ROW_F0, ROW_F1 = range(GAIN_ROWS)
GAIN_HG = GAIN_KV = 0
GAIN_F0 = GAIN_F1 = 1
GAIN_ATT = 2
PLANS = {
    0: ["R", "m", "Rm", "Rm"] + ["m"] * 10 + ["", ""],
    1: ["R", "m", "Rm", "Rm"] + ["m"] * 11 + [""],
    2: ["R", "m", "Rm", "Rm"] + ["m"] * 11 + [""],
    3: ["R", "R", "R", ""],
}


class Chain:

    def __init__(self, engine, sem):
        self.engine, self.sem, self.n, self.base, self.step = engine, sem, 0, 0, None

    def tick(self, ins):
        self.n += 1
        ins.then_inc(self.sem, 1)

    def link(self, ins):
        self.tick(ins)
        self.engine.wait_ge(self.sem, self.base + self.n if self.step is None else self.step + (self.base + self.n))

    def enter(self, i, per):
        self.base, self.n, self.per, self.step = self.base + self.n, 0, per, i * per

    def leave(self, count):
        assert self.n == self.per, self.n
        self.base, self.n, self.step = self.base + count * self.per, 0, None


class Count:

    def __init__(self):
        self.chunks = 0
        self.banks = 0
        self.transposes = 0
        self.normed = 0
        self.pairs = 0
        self.met = {}

    def next(self, name, n=1):
        self.met[name] = self.met.get(name, 0) + n
        return self.met[name]


def build(nc, x_d, wall_d, gains_d, lb_d, headg_d, rope_d, amask_d, lmask_d, ident_d, iota_d, skt_d,
          u_d, v_d, out_d):
    ctx = ExitStack()
    with ctx:
        def sb(name, shape, dt=F32):
            return ctx.enter_context(nc.sbuf_tensor(name, shape, dt))

        def sem(name):
            return ctx.enter_context(nc.semaphore(name))

        u_ring = sb("u_ring", [P, RING, D])
        v_ring = sb("v_ring", [P, RING, D])
        w_ring = sb("w_ring", [P, WRING, CHUNK])
        h = sb("h", [P, TILES, D])
        xp = sb("xp", [P, TILES, D])
        xn = sb("xn", [P, D])
        xT = sb("xT", [P, KT_D, P])
        gains = sb("gains", [P, 3, D])
        headg = sb("headg", [P, 3, HD])
        lbl = sb("lbl", [P, 2, HG_HEADS])
        lb_a = sb("lb_a", [P, HG_HEADS])
        lb_b = sb("lb_b", [P, HG_HEADS])
        rope = sb("rope", [P, TILES, 2, HALF_ROT])
        lmask = sb("lmask", [P, LEVELS + 1, P], U8)
        ident = sb("ident", [P, P])
        iota = sb("iota", [P, TOPK])
        ones = sb("ones", [P, P])
        zero = sb("zero", [P, P])
        skt = sb("skt", [P, 2, 2, N_KEYS])
        idx_all = sb("idx_all", [P, PHASES * SLOTS], U32)
        gate_all = sb("gate_all", [P, PHASES * SLOTS])
        arena = sb("arena", [P, 12 * D])

        def part(first, size):
            return arena[:, first:first + size]

        qT, kT, bT, eT, qe, ke, vi, gi, on, sT, raw, state = (part(n * D, D) for n in range(12))
        keyT = part(0, NKH * TILES * P).rearrange("p (n t) -> p n t", n=NKH)
        val = part(1536, TILES * NKH * HD).rearrange("p (t n) -> p t n", t=TILES)
        amask = part(3072, 1152)
        ks = part(4608, NKH * HD)
        qs = part(5376, NQH * HD)
        sq = part(10240, 1536)
        qhT = part(10240, NQH * P).rearrange("p (n t) -> p n t", n=NQH)
        pr = part(8192, 768)
        prT = part(8960, 768).rearrange("p (n t) -> p n t", n=6)
        oat = part(9728, 512)
        qpT = part(4608, 2048).rearrange("p (n t) -> p n t", n=2 * HEADS)
        s_all = part(8192, 2048).rearrange("p (n a k) -> p n a k", n=HEADS, a=2)

        ms = sb("ms", [P, 16])
        rs = sb("rs", [P, 16])
        rt = sb("rt", [P, 16])
        hr = sb("hr", [P, 1])
        den = sb("den", [P, 4])
        nmx = sb("nmx", [P, 4])
        rp = sb("rp", [P, 4, NQH, HALF_ROT])
        tv = sb("tv", [P, PART, 2, TOPK])
        ti = sb("ti", [P, PART, 2, TOPK], U32)
        tif = sb("tif", [P, PART, 2, TOPK])
        cand = sb("cand", [P, PART, TOPK * TOPK])
        cs = sb("cs", [P, PART, TOPK])
        ci = sb("ci", [P, PART, TOPK], U32)
        ab = sb("ab", [P, PART, 2, TOPK], U32)
        abf = sb("abf", [P, PART, 2, TOPK])
        hot = xn[:, :].rearrange("p (m n) -> p m n", n=TOPK)
        ef = sb("ef", [P, PART, 2, TOPK])
        en = sb("en", [P, PART, TOPK])
        gsum = sb("gsum", [P, PART])
        idx_cur = sb("idx_cur", [P, TOPK], U32)
        z = sb("z", [P, TOPK])
        zi = sb("zi", [P, TOPK])
        ez = sb("ez", [P, TOPK])
        gz = sb("gz", [P, TOPK])
        act_w = sb("act_w", [P, TOPK])
        diag = sb("diag", [P, RING, P])

        def pb(name, width):
            return ctx.enter_context(nc.psum_tensor(name, [P, width], F32))

        acc = pb("acc", D)
        bank = [pb("bank0", 512), pb("bank1", 512)]
        tr = pb("tr", D)
        scp = pb("scp", D)

        consts_in = sem("consts_in")
        later_in = sem("later_in")
        late_in = sem("late_in")
        gain_in = sem("gain_in")
        w_in = [sem(f"w_in{r}") for r in range(WRING)]
        w_used = sem("w_used")
        bank_read = sem("bank_read")
        u_in = [sem(f"u_in{r}") for r in range(RING)]
        v_in = [sem(f"v_in{r}") for r in range(RING)]
        u_used = sem("u_used")
        v_used = sem("v_used")
        pool_tick = sem("pool_tick")
        idx_ready = sem("idx_ready")
        idx_set = sem("idx_set")
        zi_ready = sem("zi_ready")
        ez_ready = sem("ez_ready")
        act_ready = sem("act_ready")
        diag_ready = sem("diag_ready")
        acc_done = sem("acc_done")
        acc_read = sem("acc_read")
        dve_rows = sem("dve_rows")
        dve_side = sem("dve_side")
        act_side = sem("act_side")
        to_transpose = sem("to_transpose")
        transposed = sem("transposed")
        transposes_read = sem("transposes_read")
        argument = sem("argument")
        value = sem("value")
        projected = sem("projected")
        operands = sem("operands")
        pair_full = sem("pair_full")
        pair_read = sem("pair_read")
        state_full = sem("state_full")
        state_read = sem("state_read")
        probs_ready = sem("probs_ready")
        pv_done = sem("pv_done")
        scored = sem("scored")
        cleared = sem("cleared")
        mixed = sem("mixed")
        stored = sem("stored")

        PHASE_OF = [(0, 0), (0, 1), (1, 0), (1, 1)]
        block = ctx.enter_context(nc.Block())

        def run(rows_of, mixer, route):
            def side(phase):
                yield from mixer(phase)
                yield from route(phase)

            parts = {}
            for parts[0] in side(0):
                pass
            for phase in range(PHASES):
                following = side(phase + 1) if phase + 1 < PHASES else iter(())
                plan = PLANS[phase]
                for done, kinds in enumerate(plan):
                    rows_of(phase, done, done + 1)
                    for kind in kinds:
                        if kind == "R":
                            next(parts[phase])
                        else:
                            parts[phase + 1] = next(following)
                if len(plan) < ROUNDS:
                    rows_of(phase, len(plan), ROUNDS)
                assert next(following, None) is None and next(parts[phase], None) is None

        @block.sync
        def _(sp):
            def gain(n, row):
                return gains[:, n, :], gains_d[row:row + 1, :].to_broadcast([P, D])

            for dst, src in ((h[:, 0, :], x_d[0]), gain(GAIN_HG, ROW_HG), (ident[:, :], ident_d), (lbl[:, :, :], lb_d)):
                sp.dma_start(dst, src).then_inc(consts_in, 16)
            sp.sem_inc(w_used, WRING)
            at = 0

            def stream(at, first, count):
                whole = count // WRING
                with sp.Fori(0, whole) as i:
                    for j in range(WRING):
                        sp.wait_ge(w_used, i * WRING + (at + j + 1))
                        sp.dma_start(w_ring[:, (at + j) % WRING, :],
                                     wall_d[bass.ds(i * WRING + (first + j), 1), :, :].rearrange("o p n -> p (o n)"))\
                          .then_inc(w_in[(at + j) % WRING], 16)
                for j in range(whole * WRING, count):
                    sp.wait_ge(w_used, at + j + 1)
                    sp.dma_start(w_ring[:, (at + j) % WRING, :], wall_d[first + j]).then_inc(w_in[(at + j) % WRING], 16)
                return at + count

            at = stream(at, W_IN, WRING)
            for dst, src in ((on, lmask_d), (headg[:, :, :], headg_d), gain(GAIN_F0, ROW_F0), (skt[:, :, :, :], skt_d),
                             (iota[:, :], iota_d), (h[:, 1, :], x_d[1]), gain(GAIN_ATT, ROW_ATT)):
                sp.dma_start(dst, src).then_inc(later_in, 16)
            at = stream(at, WRING, W_KV - WRING)
            at = stream(at, W_P0, W_P1 - W_P0)
            at = stream(at, W_IN, W_KV - W_IN)
            at = stream(at, W_P0, W_P1 - W_P0)
            sp.wait_ge(mixed, TILES)
            for dst, src in ((amask, amask_d), gain(GAIN_KV, ROW_KV), (rope[:, :, :, :], rope_d)):
                sp.dma_start(dst, src).then_inc(late_in, 16)
            for t in range(TILES):
                at = stream(at, W_KV, W_P0 - W_KV)
                if t == 0:
                    sp.wait_ge(acc_read, 1)
                    dst, src = gain(GAIN_F1, ROW_F1)
                    sp.dma_start(dst, src).then_inc(gain_in, 16)
                at = stream(at, W_P1, W_END - W_P1)
            for t in range(TILES):
                sp.wait_ge(acc_read, 2 + t + 1)
                sp.dma_start(out_d[t], h[:, t, :]).then_inc(stored, 16)
            sp.wait_ge(stored, 16 * TILES)

        @block.gpsimd
        def _(pool):
            nc.gpsimd.memset(arena[:, 4 * D:6 * D], 0.0).then_inc(cleared, 1)
            nc.gpsimd.memset(sT, 0.0).then_inc(cleared, 1)
            pool.sem_inc(u_used, RING)
            pool.sem_inc(v_used, RING + 1)
            with pool.Fori(0, PHASES * HEADS) as i:
                pool.wait_ge(idx_ready, i + 1)
                for g in range(GROUPS):
                    pool.wait_ge(v_used, i * TOPK + (g * RING + 1))
                    nc.gpsimd.tensor_copy(idx_cur[:, g * RING:(g + 1) * RING],
                                          idx_all[:, bass.ds(i * TOPK + g * RING, RING)]).then_inc(idx_set, 1)
                    pool.wait_ge(idx_set, i * GROUPS + (g + 1))
                    for ring, table, arrived, used, credit in ((u_ring, u_d, u_in, u_used, 0),
                                                               (v_ring, v_d, v_in, v_used, 1)):
                        for r in range(RING):
                            pool.wait_ge(used, i * TOPK + (g * RING + r + 1 + credit))
                            pool.sem_inc(pool_tick, 1)
                            nc.gpsimd.indirect_dma_start(
                                out=ring[:, r, :], out_offset=None, in_=table,
                                in_offset=bass.IndirectOffsetOnAxis(ap=idx_cur[:, g * RING + r:g * RING + r + 1], axis=0))\
                                .then_inc(arrived[r], 16)

        @block.vector
        def _(dve):
            V = nc.vector
            chain = Chain(dve, dve_side)
            rows = Chain(dve, dve_rows)
            link, tick = chain.link, chain.tick
            count = Count()

            def tt(out, a, b, op):
                return V.tensor_tensor(out, a, b, op)

            def wait_next(sem, n=1):
                dve.wait_ge(sem, count.next(sem.name, n))

            def over(ap, n):
                return ap.unsqueeze(2).to_broadcast([P, ap.shape[1], n])

            def rsqrt(n, count_of):
                y, m, t = rs[:, 0:n], ms[:, 0:n], rt[:, 0:n]
                link(V.tensor_scalar(m, m, 1.0 / count_of, EPS, ALU.mult, ALU.add))
                link(V.tensor_scalar(t.bitcast(U32), m.bitcast(U32), 1, None, ALU.logical_shift_right))
                tick(V.tensor_scalar(y.bitcast(U32), t.bitcast(U32), -1.0, RSQRT_SEED, ALU.mult, ALU.add))
                link(V.tensor_scalar(m, m, -0.5, None, ALU.mult))
                for _ in range(3):
                    link(tt(t, y, y, ALU.mult))
                    link(tt(t, t, m, ALU.mult))
                    link(V.scalar_tensor_tensor(out=y, in0=t, scalar=1.5, in1=y, op0=ALU.add, op1=ALU.mult))

            def token_rsqrt(t):
                link(V.scalar_tensor_tensor(out=xn[:, :], in0=h[:, t, :], scalar=1.0, in1=h[:, t, :],
                                            op0=ALU.mult, op1=ALU.mult, accum_out=ms[:, 0:1]))
                rsqrt(1, D)

            def head_rsqrt(src, n):
                link(V.tensor_reduce(ms[:, 0:n], src.rearrange("p (n e) -> p n e", n=n), AX.X, ALU.add))
                rsqrt(n, HD)

            def scale_gain(t, gain, dst, scale):
                link(V.scalar_tensor_tensor(out=dst, in0=h[:, t, :], scalar=scale, in1=gains[:, gain, :],
                                            op0=ALU.mult, op1=ALU.mult))
                count.transposes += 1
                count.normed = count.transposes
                dve.sem_inc(to_transpose, 1)

            def ask():
                dve.sem_inc(argument, 1)

            def answer():
                wait_next(value)

            def from_pe():
                wait_next(pair_full)

            def pair_is_read():
                dve.sem_inc(pair_read, 1)

            def gate_by(x, th):
                link(V.scalar_tensor_tensor(out=x, in0=th, scalar=1.0, in1=x, op0=ALU.add, op1=ALU.mult))

            def add_residual(t, c, chunks):
                count.chunks += chunks
                dve.wait_ge(w_used, WRING + count.chunks)
                hc = h[:, t, c * 512:(c + 1) * 512]
                link(tt(hc, hc, bank[count.banks % 2][:, :], ALU.add))
                dve.sem_inc(bank_read, 1)
                count.banks += 1

            def heads_of(a, n=HG_HEADS):
                return a.rearrange("p (n e) -> p n e", n=n)

            def hgrn(t):
                token_rsqrt(t)
                scale_gain(t, GAIN_HG, xn[:, :], rs[:, 0:1])
                yield
                yield
                wait_next(projected)
                gate_by(qT, eT)
                yield
                if t == 0:
                    dve.wait_ge(later_in, 16 * LATER)
                    link(V.tensor_copy(lmask[:, :, :].rearrange("p l t -> p (l t)"), on))
                wait_next(projected)
                for n in range(HG_HEADS):
                    c = slice(n * P, (n + 1) * P)
                    (link if n == HG_HEADS - 1 else tick)(
                        V.tensor_scalar(raw[:, c], raw[:, c], lb_b[:, n:n + 1], lb_a[:, n:n + 1], ALU.mult, ALU.add))
                ask()
                link(V.tensor_scalar(kT, raw, -1.0, 1.0, ALU.mult, ALU.add))
                dve.sem_inc(operands, 1)
                answer()
                for n in range(HG_HEADS):
                    c = slice(n * P, (n + 1) * P)
                    (link if n == HG_HEADS - 1 else tick)(
                        V.tensor_tensor_scan(bT[:, c], ones[:, :], eT[:, c], 0.0, ALU.mult, ALU.add))

                def exponents(level):
                    w = P >> level
                    b4, e4 = (a.rearrange("p (n s w) -> p n s w", s=2, w=w) for a in (bT, eT))
                    ref = b4[:, :, 0, w - 1:w].to_broadcast([P, D // (2 * w), w])
                    tick(tt(e4[:, :, 1, :], b4[:, :, 1, :], ref, ALU.subtract))
                    link(tt(e4[:, :, 0, :], ref, b4[:, :, 0, :], ALU.subtract))
                    ask()

                def decay(level, s, dst, src):
                    d, a, e = (x.rearrange("p (n s w) -> p n s w", s=2, w=P >> level)[:, :, s, :] for x in (dst, src, eT))
                    return tt(d, a, e, ALU.mult)

                exponents(1)
                if t > 0:
                    link(V.memset(sT, 0.0))
                else:
                    dve.wait_ge(cleared, 2)
                for level in range(LEVELS + 1):
                    if level < LEVELS:
                        answer()
                        q_dst, k_dst = level_buffers[(level + 1) % 2]
                        tick(decay(level + 1, 1, q_dst, qT))
                        link(decay(level + 1, 0, k_dst, kT))
                        dve.sem_inc(operands, 1)
                        if level + 2 <= LEVELS:
                            exponents(level + 2)
                    if level % 2 == 0:
                        yield
                    from_pe()
                    pair = (scp, tr)[count.pairs % 2]
                    count.pairs += 1
                    link(V.copy_predicated(heads_of(sT), lmask[:, level:level + 1, :].to_broadcast([P, HG_HEADS, P]),
                                           heads_of(pair[:, :])))
                    pair_is_read()
                if t > 0:
                    ask()
                    answer()
                    link(tt(qe, qT, eT, ALU.mult))
                dve.sem_inc(operands, 1)
                wait_next(projected)
                gate_by(gi, on)
                yield
                from_pe()
                answer()
                head_rsqrt(eT, HG_HEADS)
                link(tt(heads_of(on), heads_of(scp[:, :]), over(rs[:, 0:HG_HEADS], HD), ALU.mult))
                pair_is_read()
                count.pairs += 1
                link(tt(heads_of(on), heads_of(on), headg[:, 0:1, :].to_broadcast([P, HG_HEADS, HD]), ALU.mult))
                link(tt(on, on, gi, ALU.mult))
                dve.sem_inc(to_transpose, 1)
                count.transposes += 1
                if t == 0:
                    b3 = heads_of(bT)
                    link(tt(heads_of(eT), b3[:, :, P - 1:P].to_broadcast([P, HG_HEADS, P]), b3, ALU.subtract))
                    ask()
                    answer()
                    link(tt(ke, kT, eT, ALU.mult))
                    dve.sem_inc(to_transpose, 1)
                    count.transposes += 1
                yield
                count.chunks += 16
                count.banks += 8
                add_residual(t, 0, 2)
                add_residual(t, 1, 2)
                dve.sem_inc(mixed, 1)

            def rotate(x, n, t):
                x3 = heads_of(x, n)
                x1, x2 = x3[:, :, 0:HALF_ROT], x3[:, :, HALF_ROT:2 * HALF_ROT]
                cos, sin = (rope[:, t, m:m + 1, :].to_broadcast([P, n, HALF_ROT]) for m in range(2))
                tick(tt(rp[:, 0, 0:n, :], x1, cos, ALU.mult))
                tick(tt(rp[:, 1, 0:n, :], x2, sin, ALU.mult))
                tick(tt(rp[:, 2, 0:n, :], x2, cos, ALU.mult))
                link(tt(rp[:, 3, 0:n, :], x1, sin, ALU.mult))
                tick(tt(x1, rp[:, 0, 0:n, :], rp[:, 1, 0:n, :], ALU.subtract))
                link(tt(x2, rp[:, 2, 0:n, :], rp[:, 3, 0:n, :], ALU.add))

            def norm_heads(x, n, gain):
                link(tt(sq[:, 0:n * HD], x, x, ALU.mult))
                head_rsqrt(sq[:, 0:n * HD], n)
                link(tt(heads_of(x, n), heads_of(x, n), over(rs[:, 0:n], HD), ALU.mult))
                link(tt(heads_of(x, n), heads_of(x, n), headg[:, gain:gain + 1, :].to_broadcast([P, n, HD]), ALU.mult))

            def attention(t):
                if t == 0:
                    dve.wait_ge(late_in, 16 * LATE)
                token_rsqrt(t)
                link(V.tensor_copy(hr[:, :], rs[:, 0:1]))
                scale_gain(t, GAIN_KV, xn[:, :], hr[:, :])
                yield
                yield
                dve.wait_ge(transposed, count.transposes)
                scale_gain(t, GAIN_ATT, xn[:, :], hr[:, :])
                yield
                wait_next(projected)
                norm_heads(ks, NKH, 1)
                rotate(ks, NKH, t)
                dve.sem_inc(to_transpose, 1)
                count.transposes += 1
                yield
                wait_next(projected)
                norm_heads(qs, NQH, 2)
                rotate(qs, NQH, t)
                dve.sem_inc(to_transpose, 1)
                count.transposes += 2
                yield
                nk = P * (t + 1)
                mask = amask[:, 0:3 * P] if t == 0 else amask[:, 3 * P:9 * P]
                o = bank[(count.banks + 6) % 2]
                for j in range(NJH + 1):
                    if j > 0:
                        wait_next(pv_done)
                        link(V.reciprocal(rt[:, j:j + 1], den[:, j - 1:j]))
                        link(V.tensor_scalar(oat[:, (j - 1) * HD:j * HD], o[:, (j - 1) * HD:j * HD], rt[:, j:j + 1], None,
                                             ALU.mult))
                    if j < NJH:
                        from_pe()
                        count.pairs += 1
                        link(V.scalar_tensor_tensor(out=pr[:, 0:3 * nk], in0=scp[:, 0:3 * nk], scalar=HD ** -0.5,
                                                    in1=mask, op0=ALU.mult, op1=ALU.add))
                        pair_is_read()
                        link(V.tensor_reduce(nmx[:, j:j + 1], pr[:, 0:3 * nk], AX.X, ALU.max, negate=True))
                        ask()
                        yield
                count.transposes += NJH + 1
                dve.sem_inc(bank_read, 1)
                dve.sem_inc(to_transpose, 1)
                yield
                count.chunks += 12
                count.banks += 7
                add_residual(t, 0, 1)
                add_residual(t, 1, 1)
                dve.sem_inc(mixed, 1)

            def route_part(phase, p):
                layer, t = PHASE_OF[phase]
                lo = p * PART
                if p == 0:
                    wait_next(projected)
                dve.wait_ge(transposed, count.normed)
                pairs = [(n, a) for n in range(PART) for a in range(2)]

                def each(ops, of):
                    for op in ops:
                        for m in of:
                            (link if op is ops[-1] and m is of[-1] else tick)(op(m))

                sc = lambda m: s_all[:, lo + m[0], m[1], :]
                first = lambda a, m: a[:, m[0], m[1], 0:8]
                last = lambda a, m: a[:, m[0], m[1], 8:16]
                each([lambda m: V.max(first(tv, m), sc(m))], pairs)
                each([lambda m: V.max_index(first(ti, m), first(tv, m), sc(m)),
                      lambda m: V.match_replace(sc(m), first(tv, m), sc(m), LOWEST)], pairs)
                each([lambda m: V.max(last(tv, m), sc(m))], pairs)
                each([lambda m: V.max_index(last(ti, m), last(tv, m), sc(m))], pairs)
                for n in range(PART):
                    tick(tt(cand[:, n, :].rearrange("p (a b) -> p a b", a=TOPK), over(tv[:, n, 0, :], TOPK),
                            tv[:, n, 1:2, :].to_broadcast([P, TOPK, TOPK]), ALU.add))
                link(V.tensor_copy(tif[:, :, :, :], ti[:, :, :, :]))
                heads = list(range(PART))
                each([lambda n: V.max(cs[:, n, 0:8], cand[:, n, :])], heads)
                each([lambda n: V.max_index(ci[:, n, 0:8], cs[:, n, 0:8], cand[:, n, :]),
                      lambda n: V.match_replace(cand[:, n, :], cs[:, n, 0:8], cand[:, n, :], LOWEST)], heads)
                each([lambda n: V.max(cs[:, n, 8:16], cand[:, n, :])], heads)
                g3 = gate_all[:, phase * SLOTS + lo * TOPK:phase * SLOTS + (lo + PART) * TOPK]\
                    .rearrange("p (n k) -> p n k", n=PART)
                tick(tt(g3, cs[:, :, :], cs[:, :, 0:1].to_broadcast([P, PART, TOPK]), ALU.subtract))
                each([lambda n: V.max_index(ci[:, n, 8:16], cs[:, n, 8:16], cand[:, n, :])], heads)
                ask()
                tick(V.tensor_scalar(ab[:, :, 0, :], ci[:, :, :], 4, None, ALU.logical_shift_right))
                link(V.tensor_scalar(ab[:, :, 1, :], ci[:, :, :], TOPK - 1, None, ALU.bitwise_and))
                link(V.tensor_copy(abf[:, :, :, :], ab[:, :, :, :]))
                link(tt(hot, over(abf[:, :, :, :].rearrange("p n a k -> p (n a k)"), TOPK),
                        iota[:, :].unsqueeze(1).to_broadcast([P, 2 * PART * TOPK, TOPK]), ALU.is_equal))
                h4 = hot.rearrange("p (m k) n -> p m k n", k=TOPK)
                link(tt(h4, h4, tif[:, :, :, :].rearrange("p n a k -> p (n a) k").unsqueeze(2)
                        .to_broadcast([P, 2 * PART, TOPK, TOPK]), ALU.mult))
                link(V.tensor_reduce(ef[:, :, :, :].rearrange("p n a k -> p (n a k)"), hot, AX.X, ALU.add))
                link(V.scalar_tensor_tensor(out=en[:, :, :], in0=ef[:, :, 0, :], scalar=float(N_KEYS), in1=ef[:, :, 1, :],
                                            op0=ALU.mult, op1=ALU.add))
                V.tensor_scalar(idx_all[:, phase * SLOTS + lo * TOPK:phase * SLOTS + (lo + PART) * TOPK],
                                en[:, :, :].rearrange("p n k -> p (n k)"), float(layer * N_EXPERTS), None, ALU.add)\
                    .then_inc(idx_ready, PART)
                answer()
                link(V.tensor_reduce(gsum[:, :], g3, AX.X, ALU.add))
                link(V.reciprocal(gsum[:, :], gsum[:, :]))
                link(V.scalar_tensor_tensor(out=g3, in0=g3, scalar=0.5, in1=over(gsum[:, :], TOPK), op0=ALU.mult,
                                            op1=ALU.mult))

            def route(phase):
                layer, t = PHASE_OF[phase]
                token_rsqrt(t)
                if phase == TILES:
                    dve.wait_ge(gain_in, 16)
                scale_gain(t, (GAIN_F0, GAIN_F1)[layer], xp[:, t, :], rs[:, 0:1])
                yield
                yield
                yield
                count.chunks += 8
                count.banks += 8
                route_part(phase, 0)
                yield rest(phase)

            def rest(phase):
                for p in range(1, HEADS // PART):
                    route_part(phase, p)
                    yield

            def mixer(phase):
                layer, t = PHASE_OF[phase]
                return (attention if layer else hgrn)(t)

            def gather(phase, lo, hi):
                layer, t = PHASE_OF[phase]
                first = phase * ROUNDS + lo

                def round_of(i, n):
                    at = lambda per, value: value if i is None else i * (GROUPS * per) + value
                    g = (lo + n) % GROUPS
                    c = slice(g * RING, (g + 1) * RING)
                    for r in range(RING):
                        dve.wait_ge(u_in[r], at(16, 16 * (first + n + 1)))
                        V.scalar_tensor_tensor(out=u_ring[:, r, :], in0=u_ring[:, r, :], scalar=1.0, in1=xp[:, t, :],
                                               op0=ALU.mult, op1=ALU.mult,
                                               accum_out=z[:, g * RING + r:g * RING + r + 1]).then_inc(u_used, 1)
                    dve.wait_ge(u_used, at(RING, RING + (first + n + 1) * RING))
                    gate = (first + n) * RING
                    gate = gate_all[:, gate:gate + RING] if i is None else gate_all[:, bass.ds(i * (GROUPS * RING) + gate, RING)]
                    rows.tick(tt(gz[:, c], gate, z[:, c], ALU.mult))
                    rows.link(tt(zi[:, c], z[:, c], z[:, c], ALU.mult))
                    rows.link(V.tensor_scalar(zi[:, c], zi[:, c], GELU_CUBE, 1.0, ALU.mult, ALU.add))
                    rows.link(tt(zi[:, c], zi[:, c], z[:, c], ALU.mult))
                    dve.sem_inc(zi_ready, 1)
                    dve.wait_ge(ez_ready, at(1, first + n + 1))
                    V.scalar_tensor_tensor(out=act_w[:, c], in0=ez[:, c], scalar=1.0, in1=gz[:, c], op0=ALU.add,
                                           op1=ALU.mult).then_inc(act_ready, 1)

                if hi - lo > GROUPS:
                    with dve.Fori(0, (hi - lo) // GROUPS) as i:
                        rows.enter(i, ROW_LINKS * GROUPS)
                        for n in range(GROUPS):
                            round_of(i, n)
                    rows.leave((hi - lo) // GROUPS)
                else:
                    for n in range(hi - lo):
                        round_of(None, n)
                if hi == ROUNDS:
                    dve.wait_ge(acc_done, phase + 1)
                    tick(V.tensor_copy(h[:, t, 0:512], acc[:, 0:512]))
                    link(V.tensor_copy(h[:, t, 512:D], acc[:, 512:D]))
                    dve.sem_inc(acc_read, 1)

            level_buffers = ((qe, ke), (xn[:, :], raw))
            link(V.memset(zero[:, :], 0.0))
            link(V.memset(ones[:, :], 1.0))
            dve.wait_ge(consts_in, 16 * EARLY)
            link(tt(lb_a[:, :], lbl[:, 0, :], lbl[:, 1, :], ALU.max))
            link(tt(lbl[:, :, :], lbl[:, :, :], lb_a[:, :].unsqueeze(1).to_broadcast([P, 2, HG_HEADS]), ALU.subtract))
            ask()
            answer()
            link(tt(lb_a[:, :], lbl[:, 0, :], lbl[:, 1, :], ALU.add))
            link(V.reciprocal(lb_a[:, :], lb_a[:, :]))
            link(tt(lb_b[:, :], lbl[:, 0, :], lb_a[:, :], ALU.mult))
            link(V.tensor_scalar(lb_a[:, :], lb_b[:, :], 0.5, 0.5, ALU.mult, ALU.add))
            link(V.tensor_scalar(lb_b[:, :], lb_b[:, :], -0.5, 0.5, ALU.mult, ALU.add))
            run(gather, mixer, route)

        @block.scalar
        def _(act):
            A = nc.scalar
            chain = Chain(act, act_side)
            link, tick = chain.link, chain.tick
            count = Count()

            def wait_next(sem, n=1):
                act.wait_ge(sem, count.next(sem.name, n))

            def give(out, in_, func, **more):
                wait_next(argument)
                link(A.activation(out, in_, func, **more))
                act.sem_inc(value, 1)

            def take_transposes(*copies):
                count.transposes += 1
                act.wait_ge(transposed, count.transposes)
                for n, (dst, src) in enumerate(copies):
                    (link if n == len(copies) - 1 else tick)(A.activation(dst, src, ACT.Copy))
                act.sem_inc(transposes_read, 1)

            def take_width(dst):
                take_transposes(*((dst[:, 4 * c:4 * c + 4, :].rearrange("p n t -> p (n t)"), tr[:, c * 512:(c + 1) * 512])
                                  for c in range(2)))

            def take_bank(chunks, *moves):
                count.chunks += chunks
                act.wait_ge(w_used, WRING + count.chunks)
                source = bank[count.banks % 2]
                for n, (dst, first, width, func, scale) in enumerate(moves):
                    (link if n == len(moves) - 1 else tick)(
                        A.activation(dst, source[:, first:first + width], func, scale=scale))
                act.sem_inc(bank_read, 1)
                count.banks += 1

            def hgrn(t):
                def take_half(c, *moves):
                    s = slice(c * 512, (c + 1) * 512)
                    take_bank(2, *((dst[:, s], 0, 512, func, scale) for dst, func, scale in moves))

                tanh_of = lambda dst: (dst, ACT.Tanh, 0.5)
                take_width(xT)
                take_half(0, (qT, ACT.Copy, 0.5), tanh_of(eT))
                yield
                take_half(1, (qT, ACT.Copy, 0.5), tanh_of(eT))
                act.sem_inc(projected, 1)
                take_half(0, tanh_of(raw))
                yield
                take_half(1, tanh_of(raw))
                act.sem_inc(projected, 1)
                take_half(0, (vi, ACT.Copy, 1.0))
                yield
                give(eT, raw, ACT.Ln)
                for level in range(1, LEVELS + 1):
                    give(eT, eT, ACT.Exp)
                    if level == 2:
                        take_half(1, (vi, ACT.Copy, 1.0))
                    elif level in (4, 6):
                        take_half(level // 2 - 2, (gi, ACT.Copy, 0.5), tanh_of(on))
                    if level % 2 == 0:
                        yield
                act.sem_inc(projected, 1)
                yield
                if t > 0:
                    give(eT, bT, ACT.Exp)
                act.wait_ge(pair_full, count.next(pair_full.name, LEVELS + 2))
                link(A.activation(eT, scp[:, :], ACT.Square))
                act.sem_inc(value, 1)
                yield
                take_width(xT)
                if t == 0:
                    give(eT, eT, ACT.Exp)
                    take_width(qe.rearrange("p (n t) -> p n t", n=HG_HEADS))
                    wait_next(state_full)
                    link(A.activation(state, scp[:, :], ACT.Copy))
                    act.sem_inc(state_read, 1)
                count.chunks += 4
                count.banks += 2
                yield

            def attention(t):
                take_width(xT)
                take_bank(2, (ks[:, 0:512], 0, 512, ACT.Copy, 1.0))
                yield
                take_bank(2, (ks[:, 512:768], 0, 256, ACT.Copy, 1.0), (val[:, t, 0:256], 256, 256, ACT.Copy, 1.0))
                take_bank(2, (val[:, t, 256:768], 0, 512, ACT.Copy, 1.0))
                act.sem_inc(projected, 1)
                yield
                take_width(xT)
                take_bank(2, (qs[:, 0:512], 0, 512, ACT.Copy, 1.0))
                yield
                tokens = slice(t * P, (t + 1) * P)
                t3 = tr[:, :].rearrange("p (n t) -> p n t", n=KT_D)
                for c in range(1, 3):
                    take_bank(2, (qs[:, c * 512:(c + 1) * 512], 0, 512, ACT.Copy, 1.0))
                act.sem_inc(projected, 1)
                take_transposes((keyT[:, 0:4, tokens], t3[:, 0:4, :]), (keyT[:, 4:6, tokens], t3[:, 4:6, :]))
                yield
                take_width(qhT[:, 0:8, :])
                take_transposes((qhT[:, 8:12, :].rearrange("p n t -> p (n t)"), tr[:, 0:512]))
                yield
                nk = P * (t + 1)
                nb = 3 * (t + 1)
                for j in range(NJH):
                    wait_next(argument)
                    link(A.activation(pr[:, 0:3 * nk], pr[:, 0:3 * nk], ACT.Exp, bias=nmx[:, j:j + 1],
                                      accum_out=den[:, j:j + 1]))
                    act.sem_inc(probs_ready, 1)
                    blocks = [(0, min(4, nb))] + ([(4, nb)] if nb > 4 else [])
                    take_transposes(*((prT[:, a:b, :].rearrange("p n t -> p (n t)"), tr[:, a * P:b * P]) for a, b in blocks))
                    yield
                count.banks += 1
                take_transposes((xT[:, 0:4, :].rearrange("p n t -> p (n t)"), tr[:, 0:512]))
                count.chunks += 2
                count.banks += 2
                yield

            def route_part(phase, p):
                lo = p * PART
                g = gate_all[:, phase * SLOTS + lo * TOPK:phase * SLOTS + (lo + PART) * TOPK]
                give(g, g, ACT.Exp)

            def rest(phase):
                for p in range(1, HEADS // PART):
                    route_part(phase, p)
                    yield

            def route(phase):
                take_width(xT)
                for c in range(4):
                    take_bank(2, (qpT[:, 4 * c:4 * c + 4, :].rearrange("p n t -> p (n t)"), 0, 512, ACT.Copy, 1.0))
                    if c in (0, 2):
                        yield
                for c in range(4):
                    wait_next(scored)
                    link(A.activation(s_all[:, 2 * c:2 * c + 2, :, :].rearrange("p n a k -> p (n a k)"),
                                      bank[count.banks % 2][:, :], ACT.Copy))
                    act.sem_inc(bank_read, 1)
                    count.banks += 1
                act.sem_inc(projected, 1)
                yield
                route_part(phase, 0)
                yield rest(phase)

            def mixer(phase):
                layer, t = PHASE_OF[phase]
                return (attention if layer else hgrn)(t)

            def gather(phase, lo, hi):
                first = phase * ROUNDS + lo

                def round_of(i, n):
                    at = lambda per, value: value if i is None else i * (GROUPS * per) + value
                    g = (lo + n) % GROUPS
                    c = slice(g * RING, (g + 1) * RING)
                    act.wait_ge(zi_ready, at(1, first + n + 1))
                    A.activation(ez[:, c], zi[:, c], ACT.Tanh, scale=GELU_SCALE).then_inc(ez_ready, 1)
                    act.wait_ge(act_ready, at(1, first + n + 1))
                    for r in range(RING):
                        act.wait_ge(v_used, at(RING, (first + n) * RING + r + 2))
                        A.activation(diag[:, r, :], ident[:, :], ACT.Copy,
                                     scale=act_w[:, g * RING + r:g * RING + r + 1]).then_inc(diag_ready, 1)

                if hi - lo > GROUPS:
                    with act.Fori(0, (hi - lo) // GROUPS) as i:
                        for n in range(GROUPS):
                            round_of(i, n)
                else:
                    for n in range(hi - lo):
                        round_of(None, n)

            act.wait_ge(consts_in, 16 * EARLY)
            give(lbl[:, :, :], lbl[:, :, :], ACT.Exp)
            run(gather, mixer, route)

        @block.tensor
        def _(pe):
            M = nc.tensor.matmul
            count = Count()

            def wait_next(sem, n=1):
                pe.wait_ge(sem, count.next(sem.name, n))

            def transpose(blocks):
                if count.transposes:
                    pe.wait_ge(transposes_read, count.transposes)
                if count.pairs:
                    pe.wait_ge(pair_read, count.pairs)
                for n, src in enumerate(blocks):
                    ins = nc.tensor.transpose(tr[:, n * P:(n + 1) * P], src, ident[:, :])
                ins.then_inc(transposed, 1)
                count.transposes += 1

            def transpose_new(blocks):
                wait_next(to_transpose)
                transpose(blocks)

            def width(a):
                return [a[:, n * P:(n + 1) * P] for n in range(KT_D)]

            def take_turn():
                if count.banks >= 2:
                    pe.wait_ge(bank_read, count.banks - 1)
                count.banks += 1
                return bank[(count.banks - 1) % 2]

            def next_chunk():
                n = count.chunks
                count.chunks += 1
                pe.wait_ge(w_in[n % WRING], 16 * (n // WRING + 1))
                return w_ring[:, n % WRING, :]

            def project(turns, across):
                pe.wait_ge(transposes_read, count.transposes)
                for _ in range(turns):
                    out = take_turn()
                    for c in range(2):
                        w = next_chunk().rearrange("p (k n) -> p k n", k=KT_D)
                        if across:
                            for b in range(2):
                                for k in range(KT_D):
                                    ins = M(out[:, (2 * c + b) * P:(2 * c + b + 1) * P], w[:, k, b * P:(b + 1) * P],
                                            xT[:, k, :], start=k == 0, stop=k == KT_D - 1)
                        else:
                            for k in range(KT_D):
                                ins = M(out[:, c * 256:(c + 1) * 256], xT[:, k, :], w[:, k, :], start=k == 0,
                                        stop=k == KT_D - 1)
                        ins.then_inc(w_used, 1)

            def hgrn(t):
                def scores(level):
                    wait_next(operands)
                    if count.pairs >= 2:
                        pe.wait_ge(pair_read, count.pairs - 1)
                    pair = (scp, tr)[count.pairs % 2]
                    count.pairs += 1
                    q, k = level_buffers[level % 2] if level else (qT, kT)
                    for n in range(HG_HEADS):
                        s = slice(n * P, (n + 1) * P)
                        ins = M(pair[:, s], k[:, s], q[:, s], start=True, stop=True)
                    ins.then_inc(pair_full, 1)

                transpose_new(width(xn))
                project(1, True)
                yield
                project(2, True)
                yield
                project(1, True)
                project(1, False)
                yield
                for level in range(0, LEVELS + 1, 2):
                    scores(level)
                    if level < 6:
                        project(1, False)
                    scores(level + 1)
                    yield
                if t > 0:
                    pe.wait_ge(state_read, 1)
                wait_next(operands)
                pe.wait_ge(pair_read, count.pairs)
                wait_next(projected, 3)
                for n in range(HG_HEADS):
                    s = slice(n * P, (n + 1) * P)
                    ins = M(scp[:, s], sT[:, s], vi[:, s], start=True, stop=t == 0)
                    if t > 0:
                        ins = M(scp[:, s], qe[:, s], state[:, s], start=False, stop=True)
                ins.then_inc(pair_full, 1)
                count.pairs += 1
                yield
                transpose_new(width(on))
                if t == 0:
                    transpose_new(width(ke))
                    pe.wait_ge(transposes_read, count.transposes)
                    for n in range(HG_HEADS):
                        s = slice(n * P, (n + 1) * P)
                        ins = M(scp[:, s], qe[:, s], vi[:, s], start=True, stop=True)
                    ins.then_inc(state_full, 1)
                project(2, False)
                yield

            def attention(t):
                transpose_new(width(xn))
                project(1, False)
                yield
                project(2, False)
                yield
                transpose_new(width(xn))
                project(1, False)
                yield
                project(2, False)
                transpose_new([ks[:, n * HD:(n + 1) * HD] for n in range(NKH)])
                yield
                transpose_new([qs[:, n * HD:(n + 1) * HD] for n in range(8)])
                transpose([qs[:, n * HD:(n + 1) * HD] for n in range(8, NQH)])
                pe.wait_ge(transposes_read, count.transposes)
                nk = P * (t + 1)
                o = take_turn()

                def score(j):
                    pe.wait_ge(pair_read, count.pairs)
                    for g in range(N_GROUPS):
                        ins = M(scp[:, g * nk:(g + 1) * nk], qhT[:, g * NJH + j, :],
                                keyT[:, g * KV_PER_GROUP + j // Q_PER_KV, 0:nk], start=True, stop=True)
                    ins.then_inc(pair_full, 1)
                    count.pairs += 1

                score(0)
                yield
                for j in range(NJH):
                    if j + 1 < NJH:
                        score(j + 1)
                    wait_next(probs_ready)
                    transpose_probs([pr[:, n * P:(n + 1) * P] for n in range(3 * (t + 1))])
                    pe.wait_ge(transposes_read, count.transposes)
                    for n in range(3 * (t + 1)):
                        g, b = divmod(n, t + 1)
                        kv = g * KV_PER_GROUP + j // Q_PER_KV
                        ins = M(o[:, j * HD:(j + 1) * HD], prT[:, n, :], val[:, b, kv * HD:(kv + 1) * HD],
                                start=n == 0, stop=n == 3 * (t + 1) - 1)
                    ins.then_inc(pv_done, 1)
                    yield
                transpose_new([oat[:, n * HD:(n + 1) * HD] for n in range(NJH)])
                pe.wait_ge(transposes_read, count.transposes)
                for c in range(2):
                    out = take_turn()
                    w = next_chunk().rearrange("p (k n) -> p k n", k=4)
                    for k in range(4):
                        ins = M(out[:, :], xT[:, k, :], w[:, k, :], start=k == 0, stop=k == 3)
                    ins.then_inc(w_used, 1)
                yield

            def transpose_probs(blocks):
                pe.wait_ge(transposes_read, count.transposes)
                for n, src in enumerate(blocks):
                    ins = nc.tensor.transpose(tr[:, n * P:(n + 1) * P], src, ident[:, :])
                ins.then_inc(transposed, 1)
                count.transposes += 1

            def rest(phase):
                for p in range(1, HEADS // PART):
                    yield

            def route(phase):
                layer, t = PHASE_OF[phase]
                transpose_new([xp[:, t, n * P:(n + 1) * P] for n in range(KT_D)])
                for turns in (1, 2):
                    project(turns, True)
                    yield
                project(1, True)
                if phase == 0:
                    pe.wait_ge(later_in, 16 * LATER)
                for c in range(4):
                    out = take_turn()
                    pe.wait_ge(bank_read, count.banks - 4)
                    for b in range(4):
                        ins = M(out[:, b * P:(b + 1) * P], qpT[:, 4 * c + b, :], skt[:, layer, b % 2, :], start=True,
                                stop=True)
                    ins.then_inc(scored, 1)
                count.next(projected.name)
                yield
                yield rest(phase)

            def mixer(phase):
                layer, t = PHASE_OF[phase]
                return (attention if layer else hgrn)(t)

            level_buffers = ((qe, ke), (xn[:, :], raw))

            def gather(phase, lo, hi):
                layer, t = PHASE_OF[phase]
                first = phase * ROUNDS + lo
                halves = [slice(0, 512), slice(512, D)]

                def round_of(i, n):
                    at = lambda per, value: value if i is None else i * (GROUPS * per) + value
                    for r in range(RING):
                        pe.wait_ge(diag_ready, at(RING, (first + n) * RING + r + 1))
                        pe.wait_ge(v_in[r], at(16, 16 * (first + n + 1)))
                        for s in halves:
                            ins = M(acc[:, s], diag[:, r, :], v_ring[:, r, s], start=False, stop=False)
                        ins.then_inc(v_used, 1)

                if lo == 0:
                    pe.wait_ge(mixed, phase + 1)
                    if phase:
                        pe.wait_ge(acc_read, phase)
                    for s in halves:
                        M(acc[:, s], ident[:, :], h[:, t, s], start=True, stop=False)
                if hi - lo > GROUPS:
                    with pe.Fori(0, (hi - lo) // GROUPS) as i:
                        for n in range(GROUPS):
                            round_of(i, n)
                else:
                    for n in range(hi - lo):
                        round_of(None, n)
                if hi == ROUNDS:
                    for s in halves:
                        ins = M(acc[:, s].rearrange("p (n c) -> p n c", n=4), zero[:, :],
                                ident[:, :].unsqueeze(1).to_broadcast([P, 4, P]), start=False, stop=True)
                    ins.then_inc(acc_done, 1)

            pe.wait_ge(consts_in, 16 * EARLY)
            run(gather, mixer, route)


def kernel(**inputs):
    import numpy as np
    import concourse.bacc as bacc
    from concourse import mybir as mb
    from concourse.bass_utils import run_bass_kernel_spmd

    get = {k: np.asarray(a) for k, a in inputs.items()}

    def chunks(w, rows):
        k, n = rows // P, CHUNK // (rows // P)
        return w.reshape(k, P, w.shape[1] // n, n).transpose(2, 1, 0, 3).reshape(-1, P, CHUNK)

    pq = get["peer_w_q"]
    wall = np.concatenate([chunks(get["hgrn_w_in"][0], D), chunks(get["hgrn_w_out"][0], D), chunks(get["w_kv"], D),
                           chunks(get["w_q"][0], D), chunks(get["w_o"][0], 512), chunks(pq[0], D), chunks(pq[1], D)])
    gains = np.stack([get["hgrn_norm"][0], get["kv_norm"], get["attn_norm"][0], get["ffn_norm"][0], get["ffn_norm"][1]])
    headg = np.ascontiguousarray(np.broadcast_to(
        np.stack([get["hgrn_out_norm"][0], get["k_norm"], get["q_norm"][0]])[None], (P, 3, HD)))
    lbl = get["hgrn_lb_logits"].reshape(2, HG_HEADS, P).transpose(2, 0, 1)
    skt = get["peer_sub_keys"].transpose(3, 0, 1, 2)

    tokens = TILES * P
    inv = np.float32(500000.0) ** (-np.arange(HALF_ROT, dtype=np.float32) * np.float32(2.0) / np.float32(2 * HALF_ROT))
    ang = np.arange(tokens, dtype=np.float32)[:, None] * inv[None, :].astype(np.float32)
    rope = np.stack([np.cos(ang), np.sin(ang)], 1).astype(np.float32).reshape(TILES, P, 2, HALF_ROT).transpose(1, 0, 2, 3)
    masks = []
    for t in range(TILES):
        i, j = np.arange(P)[:, None] + t * P, np.arange((t + 1) * P)[None, :]
        for window, step in ((128, 1), (512, 4), (2048, 16)):
            ok = (i >= j) & ((i - j) % step == 0) & (i - j <= window)
            masks.append(np.where(ok, 0.0, -1.0e30).astype(np.float32))
    amask = np.concatenate(masks, 1)
    j, i = np.arange(P)[:, None], np.arange(P)[None, :]
    level_masks = [i == j]
    for level in range(1, LEVELS + 1):
        w = P >> level
        level_masks.append((i // (2 * w) == j // (2 * w)) & ((i // w) % 2 == 1) & ((j // w) % 2 == 0))
    lmask = np.stack(level_masks, 1).astype(np.float32).reshape(P, -1)
    iota = np.ascontiguousarray(np.broadcast_to(np.arange(TOPK, dtype=np.float32), (P, TOPK)))

    nc = bacc.Bacc("TRN2", target_bir_lowering=False, num_devices=1)
    arrays, args = {}, []
    for name, a in dict(
            x=get["x"].reshape(TILES, P, D), wall=wall, gains=gains, lb=lbl, headg=headg, rope=rope, amask=amask,
            lmask=lmask, ident=np.eye(P, dtype=np.float32), iota=iota, skt=skt,
            u=get["peer_u"].reshape(-1, D), v=get["peer_v"].reshape(-1, D)).items():
        a = np.ascontiguousarray(a)
        arrays[f"in_{name}"] = a
        args.append(nc.dram_tensor(f"in_{name}", a.shape, mb.dt.from_np(a.dtype), kind="ExternalInput").ap())
    args.append(nc.dram_tensor("out_0", (TILES, P, D), mb.dt.float32, kind="ExternalOutput").ap())
    build(nc, *args)
    r = run_bass_kernel_spmd(nc, [arrays], core_ids=[0])
    return r.results[0]["out_0"].reshape(1, TILES * P, D)
```

```python
import concourse.bass as bass
from concourse import mybir
from contextlib import ExitStack

F32 = mybir.dt.float32
U32 = mybir.dt.uint32
U8 = mybir.dt.uint8
ALU = mybir.AluOpType
ACT = mybir.ActivationFunctionType
AX = mybir.AxisListType

P = 128
D = 1024
KT_D = D // P
TILES = 2
EPS = 1e-6
HG_HEADS = D // P
LEVELS = 7
HD = 128
N_GROUPS, KV_PER_GROUP, Q_PER_KV = 3, 2, 2
NQH = N_GROUPS * KV_PER_GROUP * Q_PER_KV
NKH = N_GROUPS * KV_PER_GROUP
NJH = KV_PER_GROUP * Q_PER_KV
HALF_ROT = HD // 8
HEADS = 8
TOPK = 16
PART = 2
PARTS = ((0, 1), (1, 1), (2, 2), (4, 2), (6, 2))
N_KEYS = 128
N_EXPERTS = N_KEYS * N_KEYS
PHASES = 4
RING = 8
GROUPS = TOPK // RING
ROUNDS = HEADS * GROUPS
SLOTS = HEADS * TOPK
WRING = 4
CHUNK = 2048
LAST_ROWS = 2
GELU_CUBE = 0.044715
GELU_SCALE = 0.7978845608028654
LOWEST = -3.0e38
EARLY, LATER, LATE = 4, 7, 3
ROW_LINKS = 4
RSQRT_SEED = float(0x5F3759DF)

LENT = 8
W_IN, W_OUT, W_KV, W_Q, W_O, W_P0, W_P1, W_END = 0, 16, 20, 26, 32, 34, 42, 50
LENT_FIRST = W_KV + W_P1 - W_P0 - LENT
GAIN_ROWS = 5
ROW_HG, ROW_KV, ROW_ATT, ROW_F0, ROW_F1 = range(GAIN_ROWS)
GAIN_HG = GAIN_KV = 0
GAIN_F0 = GAIN_F1 = 1
GAIN_ATT = 2
PLANS = {
    0: ["R", "m", "Rm", "R"] + ["m"] * 10 + ["", ""],
    1: ["R", "m", "Rm", "R"] + ["m"] * 11 + [""],
    2: ["R", "m", "Rm", "R"] + ["m"] * 11 + [""],
    3: ["R", "R", "R", ""],
}


class Chain:

    def __init__(self, engine, sem):
        self.engine, self.sem, self.n, self.base, self.step = engine, sem, 0, 0, None

    def tick(self, ins):
        self.n += 1
        ins.then_inc(self.sem, 1)

    def link(self, ins):
        self.tick(ins)
        self.engine.wait_ge(self.sem, self.base + self.n if self.step is None else self.step + (self.base + self.n))

    def enter(self, i, per):
        self.base, self.n, self.per, self.step = self.base + self.n, 0, per, i * per

    def leave(self, count):
        assert self.n == self.per, self.n
        self.base, self.n, self.step = self.base + count * self.per, 0, None


class Count:

    def __init__(self):
        self.chunks = 0
        self.banks = 0
        self.transposes = 0
        self.normed = 0
        self.pairs = 0
        self.met = {}

    def next(self, name, n=1):
        self.met[name] = self.met.get(name, 0) + n
        return self.met[name]


def build(nc, x_d, wall_d, gains_d, lb_d, headg_d, rope_d, amask_d, lmask_d, ident_d, iota_d, skt_d,
          u_d, v_d, out_d):
    ctx = ExitStack()
    with ctx:
        def sb(name, shape, dt=F32):
            return ctx.enter_context(nc.sbuf_tensor(name, shape, dt))

        def sem(name):
            return ctx.enter_context(nc.semaphore(name))

        u_ring = sb("u_ring", [P, RING, D])
        v_ring = sb("v_ring", [P, RING, D])
        lent = [ring[:, 2 * n:2 * n + 2, :].rearrange("p r d -> p (r d)") for ring in (u_ring, v_ring)
                for n in range(LENT // 2)]
        w_ring = sb("w_ring", [P, WRING, CHUNK])
        h = sb("h", [P, TILES, D])
        xp = sb("xp", [P, TILES, D])
        xn = sb("xn", [P, D])
        xT = sb("xT", [P, KT_D, P])
        gains = sb("gains", [P, 3, D])
        headg = sb("headg", [P, 3, HD])
        lbl = sb("lbl", [P, 2, HG_HEADS])
        lb_a = sb("lb_a", [P, HG_HEADS])
        lb_b = sb("lb_b", [P, HG_HEADS])
        rope = sb("rope", [P, TILES, 2, HALF_ROT])
        lmask = sb("lmask", [P, LEVELS + 1, P], U8)
        ident = sb("ident", [P, P])
        iota = sb("iota", [P, TOPK])
        ones = sb("ones", [P, P])
        skt = sb("skt", [P, 2, 2, N_KEYS])
        idx_all = sb("idx_all", [P, PHASES * SLOTS], U32)
        gate_all = sb("gate_all", [P, PHASES * SLOTS])
        arena = sb("arena", [P, 12 * D])

        def part(first, size):
            return arena[:, first:first + size]

        qT, kT, bT, eT, qe, ke, vi, gi, on, sT, raw, state = (part(n * D, D) for n in range(12))
        keyT = part(0, NKH * TILES * P).rearrange("p (n t) -> p n t", n=NKH)
        val = part(1536, TILES * NKH * HD).rearrange("p (t n) -> p t n", t=TILES)
        amask = part(3072, 1152)
        ks = part(4608, NKH * HD)
        qs = part(5376, NQH * HD)
        sq = part(10240, 1536)
        qhT = part(10240, NQH * P).rearrange("p (n t) -> p n t", n=NQH)
        pr = part(8192, 768)
        prT = part(8960, 768).rearrange("p (n t) -> p n t", n=6)
        oat = part(9728, 512)
        qpT = part(4608, 2048).rearrange("p (n t) -> p n t", n=2 * HEADS)
        s_all = part(8192, 2048).rearrange("p (n a k) -> p n a k", n=HEADS, a=2)

        ms = sb("ms", [P, 16])
        rs = sb("rs", [P, 16])
        rt = sb("rt", [P, 16])
        hr = sb("hr", [P, 1])
        xr = sb("xr", [P, TILES])
        den = sb("den", [P, 4])
        nmx = sb("nmx", [P, 4])
        rp = sb("rp", [P, 4, NQH, HALF_ROT])
        tv = sb("tv", [P, PART, 2, TOPK])
        ti = sb("ti", [P, PART, 2, TOPK], U32)
        tif = sb("tif", [P, PART, 2, TOPK])
        cand = sb("cand", [P, PART, TOPK * TOPK])
        cs = sb("cs", [P, PART, TOPK])
        ci = sb("ci", [P, PART, TOPK], U32)
        ab = sb("ab", [P, PART, 2, TOPK], U32)
        abf = sb("abf", [P, PART, 2, TOPK])
        hot = xn[:, :].rearrange("p (m n) -> p m n", n=TOPK)
        ef = sb("ef", [P, PART, 2, TOPK])
        en = sb("en", [P, PART, TOPK])
        gsum = sb("gsum", [P, PART])
        idx_cur = sb("idx_cur", [P, TOPK], U32)
        z = sb("z", [P, TOPK])
        zi = sb("zi", [P, TOPK])
        ez = sb("ez", [P, TOPK])
        gz = sb("gz", [P, TOPK])
        act_w = sb("act_w", [P, TOPK])
        diag = sb("diag", [P, RING, P])

        def pb(name, width):
            return ctx.enter_context(nc.psum_tensor(name, [P, width], F32))

        acc = pb("acc", D)
        bank = [pb("bank0", 512), pb("bank1", 512)]
        tr = pb("tr", D)
        scp = pb("scp", D)

        consts_in = sem("consts_in")
        later_in = sem("later_in")
        late_in = sem("late_in")
        gain_in = sem("gain_in")
        w_in = [sem(f"w_in{r}") for r in range(WRING)]
        lent_in = [sem("lent_in_u"), sem("lent_in_v")]
        w_used = sem("w_used")
        bank_read = sem("bank_read")
        u_in = [sem(f"u_in{r}") for r in range(RING)]
        v_in = [sem(f"v_in{r}") for r in range(RING)]
        u_used = sem("u_used")
        v_used = sem("v_used")
        pool_tick = sem("pool_tick")
        idx_ready = sem("idx_ready")
        idx_set = sem("idx_set")
        zi_ready = sem("zi_ready")
        ez_ready = sem("ez_ready")
        act_ready = sem("act_ready")
        diag_ready = sem("diag_ready")
        acc_done = sem("acc_done")
        acc_read = sem("acc_read")
        dve_rows = sem("dve_rows")
        dve_side = sem("dve_side")
        act_side = sem("act_side")
        to_transpose = sem("to_transpose")
        transposed = sem("transposed")
        transposes_read = sem("transposes_read")
        argument = sem("argument")
        value = sem("value")
        projected = sem("projected")
        operands = sem("operands")
        pair_full = sem("pair_full")
        pair_read = sem("pair_read")
        state_full = sem("state_full")
        state_read = sem("state_read")
        probs_ready = sem("probs_ready")
        pv_done = sem("pv_done")
        scored = sem("scored")
        cleared = sem("cleared")
        factor_ready = sem("factor_ready")
        mixed = sem("mixed")
        stored = sem("stored")

        PHASE_OF = [(0, 0), (0, 1), (1, 0), (1, 1)]
        block = ctx.enter_context(nc.Block())

        def rows_for_pe(phase, n):
            return RING - LAST_ROWS if phase == PHASES - 1 and n == ROUNDS - 1 else RING

        def run(rows_of, mixer, route):
            def side(phase):
                yield from mixer(phase)
                yield from route(phase)

            parts = {}
            for parts[0] in side(0):
                pass
            for phase in range(PHASES):
                following = side(phase + 1) if phase + 1 < PHASES else iter(())
                plan = PLANS[phase]
                for done, kinds in enumerate(plan):
                    rows_of(phase, done, done + 1)
                    for kind in kinds:
                        if kind == "R":
                            next(parts[phase])
                        else:
                            parts[phase + 1] = next(following)
                if len(plan) < ROUNDS:
                    rows_of(phase, len(plan), ROUNDS - GROUPS)
                    rows_of(phase, ROUNDS - GROUPS, ROUNDS)
                assert next(following, None) is None and next(parts[phase], None) is None

        @block.sync
        def _(sp):
            def gain(n, row):
                return gains[:, n, :], gains_d[row:row + 1, :].to_broadcast([P, D])

            for dst, src in ((h[:, 0, :], x_d[0]), gain(GAIN_HG, ROW_HG), (ident[:, :], ident_d), (lbl[:, :, :], lb_d)):
                sp.dma_start(dst, src).then_inc(consts_in, 16)
            sp.sem_inc(w_used, WRING)
            at = 0

            def stream(at, first, count, lent=0):
                whole = count // WRING
                with sp.Fori(0, whole) as i:
                    for j in range(WRING):
                        sp.wait_ge(w_used, i * WRING + (at + j + 1 - lent))
                        sp.dma_start(w_ring[:, (at + j) % WRING, :],
                                     wall_d[bass.ds(i * WRING + (first + j), 1), :, :].rearrange("o p n -> p (o n)"))\
                          .then_inc(w_in[(at + j) % WRING], 16)
                for j in range(whole * WRING, count):
                    sp.wait_ge(w_used, at + j + 1 - lent)
                    sp.dma_start(w_ring[:, (at + j) % WRING, :], wall_d[first + j]).then_inc(w_in[(at + j) % WRING], 16)
                return at + count

            at = stream(at, W_IN, WRING)
            for dst, src in ((on, lmask_d), (headg[:, :, :], headg_d), gain(GAIN_F0, ROW_F0), (skt[:, :, :, :], skt_d),
                             (iota[:, :], iota_d), (h[:, 1, :], x_d[1]), gain(GAIN_ATT, ROW_ATT)):
                sp.dma_start(dst, src).then_inc(later_in, 16)
            at = stream(at, WRING, W_OUT - WRING)
            for n in range(LENT // 2):
                sp.dma_start(lent[n], wall_d[W_P1 - LENT + n]).then_inc(lent_in[0], 16)
            at = stream(at, W_OUT, W_KV - W_OUT)
            for n in range(LENT // 2, LENT):
                sp.dma_start(lent[n], wall_d[W_P1 - LENT + n]).then_inc(lent_in[1], 16)
            assert at == LENT_FIRST
            at += LENT
            at = stream(at, W_IN, WRING, LENT)
            at = stream(at, WRING, W_KV - WRING)
            at = stream(at, W_P0, W_P1 - W_P0)
            sp.wait_ge(mixed, TILES)
            for dst, src in ((amask, amask_d), gain(GAIN_KV, ROW_KV), (rope[:, :, :, :], rope_d)):
                sp.dma_start(dst, src).then_inc(late_in, 16)
            for t in range(TILES):
                at = stream(at, W_KV, W_P0 - W_KV)
                if t == 0:
                    sp.wait_ge(acc_read, 1)
                    dst, src = gain(GAIN_F1, ROW_F1)
                    sp.dma_start(dst, src).then_inc(gain_in, 16)
                at = stream(at, W_P1, W_END - W_P1)
            sp.wait_ge(acc_read, PHASES - 1)
            sp.dma_start(out_d[0], h[:, 0, :]).then_inc(stored, 16)
            for c in range(2):
                s = slice(c * 512, (c + 1) * 512)
                sp.wait_ge(acc_read, PHASES + c)
                sp.dma_start(out_d[1, :, s], h[:, 1, s]).then_inc(stored, 16)
            sp.wait_ge(stored, 16 * 3)

        @block.gpsimd
        def _(pool):
            nc.gpsimd.memset(qe, 0.0).then_inc(cleared, 1)
            nc.gpsimd.memset(sT, 0.0).then_inc(cleared, 1)
            pool.sem_inc(v_used, 1)
            with pool.Fori(0, PHASES * HEADS) as i:
                pool.wait_ge(idx_ready, i + 1)
                for g in range(GROUPS):
                    pool.wait_ge(v_used, i * TOPK + (g * RING + 1))
                    nc.gpsimd.tensor_copy(idx_cur[:, g * RING:(g + 1) * RING],
                                          idx_all[:, bass.ds(i * TOPK + g * RING, RING)]).then_inc(idx_set, 1)
                    pool.wait_ge(idx_set, i * GROUPS + (g + 1))
                    for ring, table, arrived, used, credit in ((u_ring, u_d, u_in, u_used, 0),
                                                               (v_ring, v_d, v_in, v_used, 1)):
                        for r in range(RING):
                            pool.wait_ge(used, i * TOPK + (g * RING + r + 1 + credit))
                            pool.sem_inc(pool_tick, 1)
                            nc.gpsimd.indirect_dma_start(
                                out=ring[:, r, :], out_offset=None, in_=table,
                                in_offset=bass.IndirectOffsetOnAxis(ap=idx_cur[:, g * RING + r:g * RING + r + 1], axis=0))\
                                .then_inc(arrived[r], 16)

        @block.vector
        def _(dve):
            V = nc.vector
            chain = Chain(dve, dve_side)
            rows = Chain(dve, dve_rows)
            link, tick = chain.link, chain.tick
            count = Count()

            def tt(out, a, b, op):
                return V.tensor_tensor(out, a, b, op)

            def wait_next(sem, n=1):
                dve.wait_ge(sem, count.next(sem.name, n))

            def over(ap, n):
                return ap.unsqueeze(2).to_broadcast([P, ap.shape[1], n])

            def rsqrt(n, count_of):
                y, m, t = rs[:, 0:n], ms[:, 0:n], rt[:, 0:n]
                link(V.tensor_scalar(m, m, 1.0 / count_of, EPS, ALU.mult, ALU.add))
                link(V.tensor_scalar(t.bitcast(U32), m.bitcast(U32), 1, None, ALU.logical_shift_right))
                tick(V.tensor_scalar(y.bitcast(U32), t.bitcast(U32), -1.0, RSQRT_SEED, ALU.mult, ALU.add))
                link(V.tensor_scalar(m, m, -0.5, None, ALU.mult))
                for _ in range(3):
                    link(tt(t, y, y, ALU.mult))
                    link(tt(t, t, m, ALU.mult))
                    link(V.scalar_tensor_tensor(out=y, in0=t, scalar=1.5, in1=y, op0=ALU.add, op1=ALU.mult))

            def token_rsqrt(t):
                link(V.scalar_tensor_tensor(out=xn[:, :], in0=h[:, t, :], scalar=1.0, in1=h[:, t, :],
                                            op0=ALU.mult, op1=ALU.mult, accum_out=ms[:, 0:1]))
                rsqrt(1, D)

            def head_rsqrt(src, n):
                link(V.tensor_reduce(ms[:, 0:n], src.rearrange("p (n e) -> p n e", n=n), AX.X, ALU.add))
                rsqrt(n, HD)

            def scale_gain(t, gain, dst, scale):
                link(V.scalar_tensor_tensor(out=dst, in0=h[:, t, :], scalar=scale, in1=gains[:, gain, :],
                                            op0=ALU.mult, op1=ALU.mult))
                count.transposes += 1
                count.normed = count.transposes
                dve.sem_inc(to_transpose, 1)

            def ask():
                dve.sem_inc(argument, 1)

            def answer():
                wait_next(value)

            def from_pe():
                wait_next(pair_full)

            def pair_is_read():
                dve.sem_inc(pair_read, 1)

            def gate_by(x, th):
                link(V.scalar_tensor_tensor(out=x, in0=th, scalar=1.0, in1=x, op0=ALU.add, op1=ALU.mult))

            def add_residual(t, c, chunks):
                count.chunks += chunks
                dve.wait_ge(w_used, WRING + count.chunks)
                hc = h[:, t, c * 512:(c + 1) * 512]
                link(tt(hc, hc, bank[count.banks % 2][:, :], ALU.add))
                dve.sem_inc(bank_read, 1)
                count.banks += 1

            def heads_of(a, n=HG_HEADS):
                return a.rearrange("p (n e) -> p n e", n=n)

            def lower_bound():
                link(tt(lb_a[:, :], lbl[:, 0, :], lbl[:, 1, :], ALU.max))
                link(tt(lbl[:, :, :], lbl[:, :, :], lb_a[:, :].unsqueeze(1).to_broadcast([P, 2, HG_HEADS]), ALU.subtract))
                ask()
                answer()
                link(tt(lb_a[:, :], lbl[:, 0, :], lbl[:, 1, :], ALU.add))
                link(V.reciprocal(lb_a[:, :], lb_a[:, :]))
                link(tt(lb_b[:, :], lbl[:, 0, :], lb_a[:, :], ALU.mult))
                link(V.tensor_scalar(lb_a[:, :], lb_b[:, :], 0.5, 0.5, ALU.mult, ALU.add))
                link(V.tensor_scalar(lb_b[:, :], lb_b[:, :], -0.5, 0.5, ALU.mult, ALU.add))

            def hgrn(t):
                token_rsqrt(t)
                scale_gain(t, GAIN_HG, xn[:, :], rs[:, 0:1])
                if t == 0:
                    lower_bound()
                yield
                yield
                if t == 0:
                    dve.wait_ge(later_in, 16 * LATER)
                    link(V.tensor_copy(lmask[:, :, :].rearrange("p l t -> p (l t)"), on))
                wait_next(projected)
                for n in range(HG_HEADS):
                    c = slice(n * P, (n + 1) * P)
                    (link if n == HG_HEADS - 1 else tick)(
                        V.tensor_scalar(raw[:, c], raw[:, c], lb_b[:, n:n + 1], lb_a[:, n:n + 1], ALU.mult, ALU.add))
                ask()
                link(V.tensor_scalar(kT, raw, -1.0, 1.0, ALU.mult, ALU.add))
                answer()
                for n in range(HG_HEADS):
                    c = slice(n * P, (n + 1) * P)
                    (link if n == HG_HEADS - 1 else tick)(
                        V.tensor_tensor_scan(bT[:, c], ones[:, :], eT[:, c], 0.0, ALU.mult, ALU.add))

                def exponents(level):
                    w = P >> level
                    b4, e4 = (a.rearrange("p (n s w) -> p n s w", s=2, w=w) for a in (bT, eT))
                    ref = b4[:, :, 0, w - 1:w].to_broadcast([P, D // (2 * w), w])
                    tick(tt(e4[:, :, 1, :], b4[:, :, 1, :], ref, ALU.subtract))
                    link(tt(e4[:, :, 0, :], ref, b4[:, :, 0, :], ALU.subtract))
                    ask()

                def decay(level, s, dst, src):
                    d, a, e = (x.rearrange("p (n s w) -> p n s w", s=2, w=P >> level)[:, :, s, :] for x in (dst, src, eT))
                    return tt(d, a, e, ALU.mult)

                exponents(1)
                if t > 0:
                    link(V.memset(sT, 0.0))
                else:
                    dve.wait_ge(cleared, 2)
                yield
                wait_next(projected)
                gate_by(qT, ke)
                dve.sem_inc(operands, 1)
                for level in range(LEVELS + 1):
                    if level < LEVELS:
                        answer()
                        q_dst, k_dst = level_buffers[(level + 1) % 2]
                        tick(decay(level + 1, 1, q_dst, qT))
                        link(decay(level + 1, 0, k_dst, kT))
                        dve.sem_inc(operands, 1)
                        if level + 2 <= LEVELS:
                            exponents(level + 2)
                    if level % 2 == 0:
                        yield
                    from_pe()
                    pair = (scp, tr)[count.pairs % 2]
                    count.pairs += 1
                    link(V.copy_predicated(heads_of(sT), lmask[:, level:level + 1, :].to_broadcast([P, HG_HEADS, P]),
                                           heads_of(pair[:, :])))
                    pair_is_read()
                if t > 0:
                    ask()
                    answer()
                    link(tt(qe, qT, eT, ALU.mult))
                dve.sem_inc(operands, 1)
                wait_next(projected, 2)
                gate_by(gi, on)
                link(tt(heads_of(gi), heads_of(gi), headg[:, 0:1, :].to_broadcast([P, HG_HEADS, HD]), ALU.mult))
                yield
                from_pe()
                answer()
                head_rsqrt(eT, HG_HEADS)
                link(tt(heads_of(qT), heads_of(scp[:, :]), over(rs[:, 0:HG_HEADS], HD), ALU.mult))
                pair_is_read()
                count.pairs += 1
                link(tt(on, qT, gi, ALU.mult))
                dve.sem_inc(to_transpose, 1)
                count.transposes += 1
                if t == 0:
                    b3 = heads_of(bT)
                    link(tt(heads_of(eT), b3[:, :, P - 1:P].to_broadcast([P, HG_HEADS, P]), b3, ALU.subtract))
                    ask()
                    answer()
                    link(tt(ke, kT, eT, ALU.mult))
                    dve.sem_inc(to_transpose, 1)
                    count.transposes += 1
                yield
                count.chunks += 16
                count.banks += 8
                add_residual(t, 0, 2)
                add_residual(t, 1, 2)
                dve.sem_inc(mixed, 1)

            def rotate(x, n, t):
                x3 = heads_of(x, n)
                x1, x2 = x3[:, :, 0:HALF_ROT], x3[:, :, HALF_ROT:2 * HALF_ROT]
                cos, sin = (rope[:, t, m:m + 1, :].to_broadcast([P, n, HALF_ROT]) for m in range(2))
                tick(tt(rp[:, 0, 0:n, :], x1, cos, ALU.mult))
                tick(tt(rp[:, 1, 0:n, :], x2, sin, ALU.mult))
                tick(tt(rp[:, 2, 0:n, :], x2, cos, ALU.mult))
                link(tt(rp[:, 3, 0:n, :], x1, sin, ALU.mult))
                tick(tt(x1, rp[:, 0, 0:n, :], rp[:, 1, 0:n, :], ALU.subtract))
                link(tt(x2, rp[:, 2, 0:n, :], rp[:, 3, 0:n, :], ALU.add))

            def norm_heads(x, n, gain):
                link(tt(sq[:, 0:n * HD], x, x, ALU.mult))
                head_rsqrt(sq[:, 0:n * HD], n)
                link(tt(heads_of(x, n), heads_of(x, n), over(rs[:, 0:n], HD), ALU.mult))
                link(tt(heads_of(x, n), heads_of(x, n), headg[:, gain:gain + 1, :].to_broadcast([P, n, HD]), ALU.mult))

            def attention(t):
                if t == 0:
                    dve.wait_ge(late_in, 16 * LATE)
                token_rsqrt(t)
                link(V.tensor_copy(hr[:, :], rs[:, 0:1]))
                scale_gain(t, GAIN_KV, xn[:, :], hr[:, :])
                yield
                yield
                dve.wait_ge(transposed, count.transposes)
                scale_gain(t, GAIN_ATT, xn[:, :], hr[:, :])
                yield
                wait_next(projected)
                norm_heads(ks, NKH, 1)
                rotate(ks, NKH, t)
                dve.sem_inc(to_transpose, 1)
                count.transposes += 1
                yield
                wait_next(projected)
                norm_heads(qs, NQH, 2)
                rotate(qs, NQH, t)
                dve.sem_inc(to_transpose, 1)
                count.transposes += 2
                yield
                nk = P * (t + 1)
                mask = amask[:, 0:3 * P] if t == 0 else amask[:, 3 * P:9 * P]
                o = bank[(count.banks + 6) % 2]
                for j in range(NJH + 1):
                    if j > 0:
                        wait_next(pv_done)
                        link(V.reciprocal(rt[:, j:j + 1], den[:, j - 1:j]))
                        link(V.tensor_scalar(oat[:, (j - 1) * HD:j * HD], o[:, (j - 1) * HD:j * HD], rt[:, j:j + 1], None,
                                             ALU.mult))
                    if j < NJH:
                        from_pe()
                        count.pairs += 1
                        link(V.scalar_tensor_tensor(out=pr[:, 0:3 * nk], in0=scp[:, 0:3 * nk], scalar=HD ** -0.5,
                                                    in1=mask, op0=ALU.mult, op1=ALU.add))
                        pair_is_read()
                        link(V.tensor_reduce(nmx[:, j:j + 1], pr[:, 0:3 * nk], AX.X, ALU.max, negate=True))
                        ask()
                        yield
                count.transposes += NJH + 1
                dve.sem_inc(bank_read, 1)
                dve.sem_inc(to_transpose, 1)
                yield
                count.chunks += 12
                count.banks += 7
                add_residual(t, 0, 1)
                add_residual(t, 1, 1)
                dve.sem_inc(mixed, 1)

            def route_part(phase, p):
                layer, t = PHASE_OF[phase]
                lo, heads = PARTS[p]
                if p in (0, 2):
                    wait_next(projected)
                dve.wait_ge(transposed, count.normed)
                hot_n = hot[:, 0:2 * heads * TOPK, :]
                pairs = [(n, a) for n in range(heads) for a in range(2)]

                def each(ops, of):
                    for op in ops:
                        for m in of:
                            (link if op is ops[-1] and m is of[-1] else tick)(op(m))

                sc = lambda m: s_all[:, lo + m[0], m[1], :]
                first = lambda a, m: a[:, m[0], m[1], 0:8]
                last = lambda a, m: a[:, m[0], m[1], 8:16]
                each([lambda m: V.max(first(tv, m), sc(m))], pairs)
                each([lambda m: V.max_index(first(ti, m), first(tv, m), sc(m)),
                      lambda m: V.match_replace(sc(m), first(tv, m), sc(m), LOWEST)], pairs)
                each([lambda m: V.max(last(tv, m), sc(m))], pairs)
                each([lambda m: V.max_index(last(ti, m), last(tv, m), sc(m))], pairs)
                for n in range(heads):
                    tick(tt(cand[:, n, :].rearrange("p (a b) -> p a b", a=TOPK), over(tv[:, n, 0, :], TOPK),
                            tv[:, n, 1:2, :].to_broadcast([P, TOPK, TOPK]), ALU.add))
                link(V.tensor_copy(tif[:, 0:heads, :, :], ti[:, 0:heads, :, :]))
                each([lambda n: V.max(cs[:, n, 0:8], cand[:, n, :])], range(heads))
                each([lambda n: V.max_index(ci[:, n, 0:8], cs[:, n, 0:8], cand[:, n, :]),
                      lambda n: V.match_replace(cand[:, n, :], cs[:, n, 0:8], cand[:, n, :], LOWEST)], range(heads))
                each([lambda n: V.max(cs[:, n, 8:16], cand[:, n, :])], range(heads))
                g3 = gate_all[:, phase * SLOTS + lo * TOPK:phase * SLOTS + (lo + heads) * TOPK]\
                    .rearrange("p (n k) -> p n k", n=heads)
                tick(tt(g3, cs[:, 0:heads, :], cs[:, 0:heads, 0:1].to_broadcast([P, heads, TOPK]), ALU.subtract))
                each([lambda n: V.max_index(ci[:, n, 8:16], cs[:, n, 8:16], cand[:, n, :])], range(heads))
                ask()
                tick(V.tensor_scalar(ab[:, 0:heads, 0, :], ci[:, 0:heads, :], 4, None, ALU.logical_shift_right))
                link(V.tensor_scalar(ab[:, 0:heads, 1, :], ci[:, 0:heads, :], TOPK - 1, None, ALU.bitwise_and))
                link(V.tensor_copy(abf[:, 0:heads, :, :], ab[:, 0:heads, :, :]))
                link(tt(hot_n, over(abf[:, 0:heads, :, :].rearrange("p n a k -> p (n a k)"), TOPK),
                        iota[:, :].unsqueeze(1).to_broadcast([P, 2 * heads * TOPK, TOPK]), ALU.is_equal))
                h4 = hot_n.rearrange("p (m k) n -> p m k n", k=TOPK)
                link(tt(h4, h4, tif[:, 0:heads, :, :].rearrange("p n a k -> p (n a) k").unsqueeze(2)
                        .to_broadcast([P, 2 * heads, TOPK, TOPK]), ALU.mult))
                link(V.tensor_reduce(ef[:, 0:heads, :, :].rearrange("p n a k -> p (n a k)"), hot_n, AX.X, ALU.add))
                link(V.scalar_tensor_tensor(out=en[:, 0:heads, :], in0=ef[:, 0:heads, 0, :], scalar=float(N_KEYS),
                                            in1=ef[:, 0:heads, 1, :],
                                            op0=ALU.mult, op1=ALU.add))
                V.tensor_scalar(idx_all[:, phase * SLOTS + lo * TOPK:phase * SLOTS + (lo + heads) * TOPK],
                                en[:, 0:heads, :].rearrange("p n k -> p (n k)"), float(layer * N_EXPERTS), None, ALU.add)\
                    .then_inc(idx_ready, heads)
                answer()
                link(V.tensor_reduce(gsum[:, 0:heads], g3, AX.X, ALU.add))
                link(V.reciprocal(gsum[:, 0:heads], gsum[:, 0:heads]))
                link(V.scalar_tensor_tensor(out=g3, in0=g3, scalar=0.5, in1=over(gsum[:, 0:heads], TOPK), op0=ALU.mult,
                                            op1=ALU.mult))

            def route(phase):
                layer, t = PHASE_OF[phase]
                if phase == TILES:
                    dve.wait_ge(gain_in, 16)
                scale_gain(t, (GAIN_F0, GAIN_F1)[layer], xp[:, t, :], 1.0)
                token_rsqrt(t)
                link(V.tensor_copy(xr[:, t:t + 1], rs[:, 0:1]))
                dve.sem_inc(factor_ready, 1)
                yield
                dve.wait_ge(transposed, count.normed)
                link(V.tensor_scalar(xp[:, t, :], xp[:, t, :], xr[:, t:t + 1], None, ALU.mult))
                count.chunks += 8
                count.banks += 8
                route_part(phase, 0)
                yield
                route_part(phase, 1)
                yield rest(phase)

            def rest(phase):
                for p in range(2, len(PARTS)):
                    route_part(phase, p)
                    yield

            def mixer(phase):
                layer, t = PHASE_OF[phase]
                return (attention if layer else hgrn)(t)

            def gather(phase, lo, hi):
                layer, t = PHASE_OF[phase]
                first = phase * ROUNDS + lo

                def round_of(i, n):
                    at = lambda per, value: value if i is None else i * (GROUPS * per) + value
                    g = (lo + n) % GROUPS
                    c = slice(g * RING, (g + 1) * RING)
                    for r in range(RING):
                        dve.wait_ge(u_in[r], at(16, 16 * (first + n + 1)))
                        V.scalar_tensor_tensor(out=u_ring[:, r, :], in0=u_ring[:, r, :], scalar=1.0, in1=xp[:, t, :],
                                               op0=ALU.mult, op1=ALU.mult,
                                               accum_out=z[:, g * RING + r:g * RING + r + 1]).then_inc(u_used, 1)
                    dve.wait_ge(u_used, at(RING, RING + (first + n + 1) * RING))
                    gate = (first + n) * RING
                    gate = gate_all[:, gate:gate + RING] if i is None else gate_all[:, bass.ds(i * (GROUPS * RING) + gate, RING)]
                    rows.tick(tt(gz[:, c], gate, z[:, c], ALU.mult))
                    rows.link(tt(zi[:, c], z[:, c], z[:, c], ALU.mult))
                    rows.link(V.tensor_scalar(zi[:, c], zi[:, c], GELU_CUBE, 1.0, ALU.mult, ALU.add))
                    rows.link(tt(zi[:, c], zi[:, c], z[:, c], ALU.mult))
                    dve.sem_inc(zi_ready, 1)
                    dve.wait_ge(ez_ready, at(1, first + n + 1))
                    V.scalar_tensor_tensor(out=act_w[:, c], in0=ez[:, c], scalar=1.0, in1=gz[:, c], op0=ALU.add,
                                           op1=ALU.mult).then_inc(act_ready, 1)

                if hi - lo > GROUPS:
                    with dve.Fori(0, (hi - lo) // GROUPS) as i:
                        rows.enter(i, ROW_LINKS * GROUPS)
                        for n in range(GROUPS):
                            round_of(i, n)
                    rows.leave((hi - lo) // GROUPS)
                else:
                    for n in range(hi - lo):
                        round_of(None, n)
                if hi == ROUNDS and phase + 1 < PHASES:
                    dve.wait_ge(acc_done, phase + 1)
                    tick(V.tensor_copy(h[:, t, 0:512], acc[:, 0:512]))
                    link(V.tensor_copy(h[:, t, 512:D], acc[:, 512:D]))
                    dve.sem_inc(acc_read, 1)
                elif hi == ROUNDS:
                    r0 = RING - LAST_ROWS
                    last = v_ring[:, r0, :]
                    weight = lambda r: act_w[:, TOPK - RING + r:TOPK - RING + r + 1]
                    dve.wait_ge(act_ready, PHASES * ROUNDS)
                    dve.wait_ge(v_in[r0], 16 * PHASES * ROUNDS)
                    link(V.tensor_scalar(last, last, weight(r0), None, ALU.mult))
                    for r in range(r0 + 1, RING):
                        dve.wait_ge(v_in[r], 16 * PHASES * ROUNDS)
                        link(V.scalar_tensor_tensor(out=last, in0=v_ring[:, r, :], scalar=weight(r), in1=last,
                                                    op0=ALU.mult, op1=ALU.add))
                    dve.wait_ge(acc_done, phase + 1)
                    for c in range(2):
                        s = slice(c * 512, (c + 1) * 512)
                        link(tt(h[:, t, s], acc[:, s], last[:, s], ALU.add))
                        dve.sem_inc(acc_read, 1)

            level_buffers = ((qe, ke), (xn[:, :], raw))
            link(V.memset(ones[:, :], 1.0))
            dve.wait_ge(consts_in, 16 * EARLY)
            run(gather, mixer, route)

        @block.scalar
        def _(act):
            A = nc.scalar
            chain = Chain(act, act_side)
            link, tick = chain.link, chain.tick
            count = Count()

            def wait_next(sem, n=1):
                act.wait_ge(sem, count.next(sem.name, n))

            def give(out, in_, func, **more):
                wait_next(argument)
                link(A.activation(out, in_, func, **more))
                act.sem_inc(value, 1)

            def take_transposes(*copies):
                count.transposes += 1
                act.wait_ge(transposed, count.transposes)
                for n, (dst, src) in enumerate(copies):
                    (link if n == len(copies) - 1 else tick)(A.activation(dst, src, ACT.Copy))
                act.sem_inc(transposes_read, 1)

            def take_width(dst):
                take_transposes(*((dst[:, 4 * c:4 * c + 4, :].rearrange("p n t -> p (n t)"), tr[:, c * 512:(c + 1) * 512])
                                  for c in range(2)))

            def take_bank(chunks, *moves):
                count.chunks += chunks
                act.wait_ge(w_used, WRING + count.chunks)
                source = bank[count.banks % 2]
                for n, (dst, first, width, func, scale) in enumerate(moves):
                    (link if n == len(moves) - 1 else tick)(
                        A.activation(dst, source[:, first:first + width], func, scale=scale))
                act.sem_inc(bank_read, 1)
                count.banks += 1

            def hgrn(t):
                def take_half(c, *moves):
                    s = slice(c * 512, (c + 1) * 512)
                    take_bank(2, *((dst[:, s], 0, 512, func, scale) for dst, func, scale in moves))

                tanh_of = lambda dst: (dst, ACT.Tanh, 0.5)
                take_width(xT)
                take_half(0, tanh_of(raw))
                yield
                take_half(1, tanh_of(raw))
                act.sem_inc(projected, 1)
                take_half(0, (qT, ACT.Copy, 0.5), tanh_of(ke))
                yield
                give(eT, raw, ACT.Ln)
                give(eT, eT, ACT.Exp)
                take_half(1, (qT, ACT.Copy, 0.5), tanh_of(ke))
                act.sem_inc(projected, 1)
                take_half(0, (vi, ACT.Copy, 1.0))
                yield
                for level in range(2, LEVELS + 1):
                    give(eT, eT, ACT.Exp)
                    if level == 4:
                        take_half(1, (vi, ACT.Copy, 1.0))
                        act.sem_inc(projected, 1)
                    elif level == 6:
                        take_half(0, (gi, ACT.Copy, 0.5), tanh_of(on))
                    if level % 2 == 0:
                        yield
                take_half(1, (gi, ACT.Copy, 0.5), tanh_of(on))
                act.sem_inc(projected, 1)
                yield
                if t > 0:
                    give(eT, bT, ACT.Exp)
                act.wait_ge(pair_full, count.next(pair_full.name, LEVELS + 2))
                link(A.activation(eT, scp[:, :], ACT.Square))
                act.sem_inc(value, 1)
                yield
                take_width(xT)
                count.chunks += 4
                count.banks += 2
                if t == 0:
                    give(eT, eT, ACT.Exp)
                    take_width(qe.rearrange("p (n t) -> p n t", n=HG_HEADS))
                    wait_next(state_full)
                    link(A.activation(state, scp[:, :], ACT.Copy))
                    act.sem_inc(state_read, 1)
                yield

            def attention(t):
                take_width(xT)
                take_bank(2, (ks[:, 0:512], 0, 512, ACT.Copy, 1.0))
                yield
                take_bank(2, (ks[:, 512:768], 0, 256, ACT.Copy, 1.0), (val[:, t, 0:256], 256, 256, ACT.Copy, 1.0))
                take_bank(2, (val[:, t, 256:768], 0, 512, ACT.Copy, 1.0))
                act.sem_inc(projected, 1)
                yield
                take_width(xT)
                take_bank(2, (qs[:, 0:512], 0, 512, ACT.Copy, 1.0))
                yield
                tokens = slice(t * P, (t + 1) * P)
                t3 = tr[:, :].rearrange("p (n t) -> p n t", n=KT_D)
                for c in range(1, 3):
                    take_bank(2, (qs[:, c * 512:(c + 1) * 512], 0, 512, ACT.Copy, 1.0))
                act.sem_inc(projected, 1)
                take_transposes((keyT[:, 0:4, tokens], t3[:, 0:4, :]), (keyT[:, 4:6, tokens], t3[:, 4:6, :]))
                yield
                take_width(qhT[:, 0:8, :])
                take_transposes((qhT[:, 8:12, :].rearrange("p n t -> p (n t)"), tr[:, 0:512]))
                yield
                nk = P * (t + 1)
                nb = 3 * (t + 1)
                for j in range(NJH):
                    wait_next(argument)
                    link(A.activation(pr[:, 0:3 * nk], pr[:, 0:3 * nk], ACT.Exp, bias=nmx[:, j:j + 1],
                                      accum_out=den[:, j:j + 1]))
                    act.sem_inc(probs_ready, 1)
                    blocks = [(0, min(4, nb))] + ([(4, nb)] if nb > 4 else [])
                    take_transposes(*((prT[:, a:b, :].rearrange("p n t -> p (n t)"), tr[:, a * P:b * P]) for a, b in blocks))
                    yield
                count.banks += 1
                take_transposes((xT[:, 0:4, :].rearrange("p n t -> p (n t)"), tr[:, 0:512]))
                count.chunks += 2
                count.banks += 2
                yield

            def route_part(phase, p):
                lo, heads = PARTS[p]
                g = gate_all[:, phase * SLOTS + lo * TOPK:phase * SLOTS + (lo + heads) * TOPK]
                give(g, g, ACT.Exp)

            def rest(phase):
                for p in range(2, len(PARTS)):
                    route_part(phase, p)
                    yield

            def route(phase):
                layer, t = PHASE_OF[phase]

                def queries(c):
                    take_bank(2, (qpT[:, 4 * c:4 * c + 4, :].rearrange("p n t -> p (n t)"), 0, 512, ACT.Copy, 1.0))

                def scores(c):
                    wait_next(scored)
                    act.wait_ge(factor_ready, phase + 1)
                    link(A.activation(s_all[:, 2 * c:2 * c + 2, :, :].rearrange("p n a k -> p (n a k)"),
                                      bank[count.banks % 2][:, :], ACT.Copy, scale=xr[:, t:t + 1]))
                    act.sem_inc(bank_read, 1)
                    count.banks += 1

                take_width(xT)
                queries(0)
                scores(0)
                act.sem_inc(projected, 1)
                yield
                route_part(phase, 0)
                queries(1)
                queries(2)
                scores(1)
                scores(2)
                yield
                route_part(phase, 1)
                queries(3)
                scores(3)
                act.sem_inc(projected, 1)
                yield rest(phase)

            def mixer(phase):
                layer, t = PHASE_OF[phase]
                return (attention if layer else hgrn)(t)

            def gather(phase, lo, hi):
                first = phase * ROUNDS + lo

                def round_of(i, n):
                    at = lambda per, value: value if i is None else i * (GROUPS * per) + value
                    g = (lo + n) % GROUPS
                    c = slice(g * RING, (g + 1) * RING)
                    act.wait_ge(zi_ready, at(1, first + n + 1))
                    A.activation(ez[:, c], zi[:, c], ACT.Tanh, scale=GELU_SCALE).then_inc(ez_ready, 1)
                    act.wait_ge(act_ready, at(1, first + n + 1))
                    for r in range(rows_for_pe(phase, lo + n)):
                        act.wait_ge(v_used, at(RING, (first + n) * RING + r + 2))
                        A.activation(diag[:, r, :], ident[:, :], ACT.Copy,
                                     scale=act_w[:, g * RING + r:g * RING + r + 1]).then_inc(diag_ready, 1)

                if hi - lo > GROUPS:
                    with act.Fori(0, (hi - lo) // GROUPS) as i:
                        for n in range(GROUPS):
                            round_of(i, n)
                else:
                    for n in range(hi - lo):
                        round_of(None, n)

            act.wait_ge(consts_in, 16 * EARLY)
            give(lbl[:, :, :], lbl[:, :, :], ACT.Exp)
            run(gather, mixer, route)

        @block.tensor
        def _(pe):
            M = nc.tensor.matmul
            count = Count()

            def wait_next(sem, n=1):
                pe.wait_ge(sem, count.next(sem.name, n))

            def transpose(blocks):
                if count.transposes:
                    pe.wait_ge(transposes_read, count.transposes)
                if count.pairs:
                    pe.wait_ge(pair_read, count.pairs)
                for n, src in enumerate(blocks):
                    ins = nc.tensor.transpose(tr[:, n * P:(n + 1) * P], src, ident[:, :])
                ins.then_inc(transposed, 1)
                count.transposes += 1

            def transpose_new(blocks):
                wait_next(to_transpose)
                transpose(blocks)

            def width(a):
                return [a[:, n * P:(n + 1) * P] for n in range(KT_D)]

            def take_turn():
                if count.banks >= 2:
                    pe.wait_ge(bank_read, count.banks - 1)
                count.banks += 1
                return bank[(count.banks - 1) % 2]

            def next_chunk():
                n = count.chunks
                count.chunks += 1
                if LENT_FIRST <= n < LENT_FIRST + LENT:
                    pe.wait_ge(lent_in[2 * (n - LENT_FIRST) // LENT], 16 * (LENT // 2))
                    return lent[n - LENT_FIRST]
                pe.wait_ge(w_in[n % WRING], 16 * (n // WRING + (1 if n < LENT_FIRST else 1 - LENT // WRING)))
                return w_ring[:, n % WRING, :]

            def project(turns, across):
                pe.wait_ge(transposes_read, count.transposes)
                for _ in range(turns):
                    out = take_turn()
                    for c in range(2):
                        w = next_chunk().rearrange("p (k n) -> p k n", k=KT_D)
                        if across:
                            for b in range(2):
                                for k in range(KT_D):
                                    ins = M(out[:, (2 * c + b) * P:(2 * c + b + 1) * P], w[:, k, b * P:(b + 1) * P],
                                            xT[:, k, :], start=k == 0, stop=k == KT_D - 1)
                        else:
                            for k in range(KT_D):
                                ins = M(out[:, c * 256:(c + 1) * 256], xT[:, k, :], w[:, k, :], start=k == 0,
                                        stop=k == KT_D - 1)
                        ins.then_inc(w_used, 1)

            def hgrn(t):
                def scores(level):
                    wait_next(operands)
                    if count.pairs >= 2:
                        pe.wait_ge(pair_read, count.pairs - 1)
                    pair = (scp, tr)[count.pairs % 2]
                    count.pairs += 1
                    q, k = level_buffers[level % 2] if level else (qT, kT)
                    for n in range(HG_HEADS):
                        s = slice(n * P, (n + 1) * P)
                        ins = M(pair[:, s], k[:, s], q[:, s], start=True, stop=True)
                    ins.then_inc(pair_full, 1)

                transpose_new(width(xn))
                project(1, True)
                yield
                project(2, True)
                yield
                project(1, True)
                project(1, False)
                yield
                for level in range(0, LEVELS + 1, 2):
                    scores(level)
                    if level == 6:
                        project(1, False)
                    scores(level + 1)
                    if level < 4:
                        project(1, False)
                    yield
                if t > 0:
                    pe.wait_ge(state_read, 1)
                wait_next(operands)
                pe.wait_ge(pair_read, count.pairs)
                wait_next(projected, 3)
                for n in range(HG_HEADS):
                    s = slice(n * P, (n + 1) * P)
                    ins = M(scp[:, s], sT[:, s], vi[:, s], start=True, stop=t == 0)
                    if t > 0:
                        ins = M(scp[:, s], qe[:, s], state[:, s], start=False, stop=True)
                ins.then_inc(pair_full, 1)
                count.pairs += 1
                count.next(projected.name)
                yield
                transpose_new(width(on))
                project(2, False)
                if t == 0:
                    transpose_new(width(ke))
                    pe.wait_ge(transposes_read, count.transposes)
                    for n in range(HG_HEADS):
                        s = slice(n * P, (n + 1) * P)
                        ins = M(scp[:, s], qe[:, s], vi[:, s], start=True, stop=True)
                    ins.then_inc(state_full, 1)
                yield

            def attention(t):
                transpose_new(width(xn))
                project(1, False)
                yield
                project(2, False)
                yield
                transpose_new(width(xn))
                project(1, False)
                yield
                project(2, False)
                transpose_new([ks[:, n * HD:(n + 1) * HD] for n in range(NKH)])
                yield
                transpose_new([qs[:, n * HD:(n + 1) * HD] for n in range(8)])
                transpose([qs[:, n * HD:(n + 1) * HD] for n in range(8, NQH)])
                pe.wait_ge(transposes_read, count.transposes)
                nk = P * (t + 1)
                o = take_turn()

                def score(j):
                    pe.wait_ge(pair_read, count.pairs)
                    for g in range(N_GROUPS):
                        ins = M(scp[:, g * nk:(g + 1) * nk], qhT[:, g * NJH + j, :],
                                keyT[:, g * KV_PER_GROUP + j // Q_PER_KV, 0:nk], start=True, stop=True)
                    ins.then_inc(pair_full, 1)
                    count.pairs += 1

                score(0)
                yield
                for j in range(NJH):
                    if j + 1 < NJH:
                        score(j + 1)
                    wait_next(probs_ready)
                    transpose_probs([pr[:, n * P:(n + 1) * P] for n in range(3 * (t + 1))])
                    pe.wait_ge(transposes_read, count.transposes)
                    for n in range(3 * (t + 1)):
                        g, b = divmod(n, t + 1)
                        kv = g * KV_PER_GROUP + j // Q_PER_KV
                        ins = M(o[:, j * HD:(j + 1) * HD], prT[:, n, :], val[:, b, kv * HD:(kv + 1) * HD],
                                start=n == 0, stop=n == 3 * (t + 1) - 1)
                    ins.then_inc(pv_done, 1)
                    yield
                transpose_new([oat[:, n * HD:(n + 1) * HD] for n in range(NJH)])
                pe.wait_ge(transposes_read, count.transposes)
                for c in range(2):
                    out = take_turn()
                    w = next_chunk().rearrange("p (k n) -> p k n", k=4)
                    for k in range(4):
                        ins = M(out[:, :], xT[:, k, :], w[:, k, :], start=k == 0, stop=k == 3)
                    ins.then_inc(w_used, 1)
                yield

            def transpose_probs(blocks):
                pe.wait_ge(transposes_read, count.transposes)
                for n, src in enumerate(blocks):
                    ins = nc.tensor.transpose(tr[:, n * P:(n + 1) * P], src, ident[:, :])
                ins.then_inc(transposed, 1)
                count.transposes += 1

            def rest(phase):
                for p in range(2, len(PARTS)):
                    yield

            def route(phase):
                layer, t = PHASE_OF[phase]
                transpose_new([xp[:, t, n * P:(n + 1) * P] for n in range(KT_D)])
                turn_of = {}

                def queries(c):
                    project(1, True)
                    turn_of[c] = count.banks

                def scores(c):
                    out = take_turn()
                    pe.wait_ge(bank_read, turn_of[c])
                    for b in range(4):
                        ins = M(out[:, b * P:(b + 1) * P], qpT[:, 4 * c + b, :], skt[:, layer, b % 2, :], start=True,
                                stop=True)
                    ins.then_inc(scored, 1)

                queries(0)
                if phase == 0:
                    pe.wait_ge(later_in, 16 * LATER)
                scores(0)
                yield
                queries(1)
                if phase == 0:
                    pe.wait_ge(w_used, WRING + count.chunks)
                    pe.sem_inc(u_used, RING)
                queries(2)
                scores(1)
                scores(2)
                yield
                queries(3)
                if phase == 0:
                    pe.wait_ge(w_used, WRING + count.chunks)
                    pe.sem_inc(v_used, RING)
                scores(3)
                count.next(projected.name, 2)
                yield rest(phase)

            def mixer(phase):
                layer, t = PHASE_OF[phase]
                return (attention if layer else hgrn)(t)

            level_buffers = ((qe, ke), (xn[:, :], raw))

            def gather(phase, lo, hi):
                layer, t = PHASE_OF[phase]
                first = phase * ROUNDS + lo
                halves = [slice(0, 512), slice(512, D)]

                def round_of(i, n):
                    at = lambda per, value: value if i is None else i * (GROUPS * per) + value
                    count_of = rows_for_pe(phase, lo + n)
                    for r in range(count_of):
                        pe.wait_ge(diag_ready, at(RING, (first + n) * RING + r + 1))
                        pe.wait_ge(v_in[r], at(16, 16 * (first + n + 1)))
                        for s in halves:
                            ins = M(acc[:, s], diag[:, r, :], v_ring[:, r, s], start=False,
                                    stop=hi == ROUNDS and n == hi - lo - 1 and r == count_of - 1)
                        ins.then_inc(v_used, 1)

                if lo == 0:
                    pe.wait_ge(mixed, phase + 1)
                    if phase:
                        pe.wait_ge(acc_read, phase)
                    for s in halves:
                        M(acc[:, s], ident[:, :], h[:, t, s], start=True, stop=False)
                if hi - lo > GROUPS:
                    with pe.Fori(0, (hi - lo) // GROUPS) as i:
                        for n in range(GROUPS):
                            round_of(i, n)
                else:
                    for n in range(hi - lo):
                        round_of(None, n)
                if hi == ROUNDS:
                    pe.wait_ge(v_used, 1 + RING + SLOTS * (phase + 1) - (RING - rows_for_pe(phase, ROUNDS - 1)))
                    pe.sem_inc(acc_done, 1)

            pe.wait_ge(consts_in, 16 * EARLY)
            run(gather, mixer, route)


def kernel(**inputs):
    import numpy as np
    import concourse.bacc as bacc
    from concourse import mybir as mb
    from concourse.bass_utils import run_bass_kernel_spmd

    get = {k: np.asarray(a) for k, a in inputs.items()}

    def chunks(w, rows):
        k, n = rows // P, CHUNK // (rows // P)
        return w.reshape(k, P, w.shape[1] // n, n).transpose(2, 1, 0, 3).reshape(-1, P, CHUNK)

    pq = get["peer_w_q"]
    w_q, w_f, w_rest = np.split(get["hgrn_w_in"][0], [D, 2 * D], axis=1)
    wall = np.concatenate([chunks(np.concatenate([w_f, w_q, w_rest], 1), D), chunks(get["hgrn_w_out"][0], D), chunks(get["w_kv"], D),
                           chunks(get["w_q"][0], D), chunks(get["w_o"][0], 512), chunks(pq[0], D), chunks(pq[1], D)])
    gains = np.stack([get["hgrn_norm"][0], get["kv_norm"], get["attn_norm"][0], get["ffn_norm"][0], get["ffn_norm"][1]])
    headg = np.ascontiguousarray(np.broadcast_to(
        np.stack([get["hgrn_out_norm"][0], get["k_norm"], get["q_norm"][0]])[None], (P, 3, HD)))
    lbl = get["hgrn_lb_logits"].reshape(2, HG_HEADS, P).transpose(2, 0, 1)
    skt = get["peer_sub_keys"].transpose(3, 0, 1, 2)

    tokens = TILES * P
    inv = np.float32(500000.0) ** (-np.arange(HALF_ROT, dtype=np.float32) * np.float32(2.0) / np.float32(2 * HALF_ROT))
    ang = np.arange(tokens, dtype=np.float32)[:, None] * inv[None, :].astype(np.float32)
    rope = np.stack([np.cos(ang), np.sin(ang)], 1).astype(np.float32).reshape(TILES, P, 2, HALF_ROT).transpose(1, 0, 2, 3)
    masks = []
    for t in range(TILES):
        i, j = np.arange(P)[:, None] + t * P, np.arange((t + 1) * P)[None, :]
        for window, step in ((128, 1), (512, 4), (2048, 16)):
            ok = (i >= j) & ((i - j) % step == 0) & (i - j <= window)
            masks.append(np.where(ok, 0.0, -1.0e30).astype(np.float32))
    amask = np.concatenate(masks, 1)
    j, i = np.arange(P)[:, None], np.arange(P)[None, :]
    level_masks = [i == j]
    for level in range(1, LEVELS + 1):
        w = P >> level
        level_masks.append((i // (2 * w) == j // (2 * w)) & ((i // w) % 2 == 1) & ((j // w) % 2 == 0))
    lmask = np.stack(level_masks, 1).astype(np.float32).reshape(P, -1)
    iota = np.ascontiguousarray(np.broadcast_to(np.arange(TOPK, dtype=np.float32), (P, TOPK)))

    nc = bacc.Bacc("TRN2", target_bir_lowering=False, num_devices=1)
    arrays, args = {}, []
    for name, a in dict(
            x=get["x"].reshape(TILES, P, D), wall=wall, gains=gains, lb=lbl, headg=headg, rope=rope, amask=amask,
            lmask=lmask, ident=np.eye(P, dtype=np.float32), iota=iota, skt=skt,
            u=get["peer_u"].reshape(-1, D), v=get["peer_v"].reshape(-1, D)).items():
        a = np.ascontiguousarray(a)
        arrays[f"in_{name}"] = a
        args.append(nc.dram_tensor(f"in_{name}", a.shape, mb.dt.from_np(a.dtype), kind="ExternalInput").ap())
    args.append(nc.dram_tensor("out_0", (TILES, P, D), mb.dt.float32, kind="ExternalOutput").ap())
    build(nc, *args)
    r = run_bass_kernel_spmd(nc, [arrays], core_ids=[0])
    return r.results[0]["out_0"].reshape(1, TILES * P, D)
```
